# Optimizing a Trainium2 kernel written in Bass

```python
import jax, jax.numpy as jnp
from jax import lax
import numpy as np

D_MODEL = 2048
BATCH = 1
SEQ = 256
DEPTH = 2

N_MIXERS = 2
N_A = (DEPTH + N_MIXERS - 1) // N_MIXERS
N_B = DEPTH // N_MIXERS
EPS = 1e-6
ROPE_THETA = 10000.0

A_HEADS = 16
A_HEAD_DIM = D_MODEL // A_HEADS
A_Q_WIDTH = A_HEADS * A_HEAD_DIM
IDX_HEADS = 16
IDX_DIM = 64
TOPK_MAX = 256
Q_BLOCK = 128
A_OFF_K = A_Q_WIDTH
A_OFF_V = A_OFF_K + A_HEAD_DIM
A_OFF_QI = A_OFF_V + A_HEAD_DIM
A_OFF_KI = A_OFF_QI + IDX_HEADS * IDX_DIM
A_OFF_WI = A_OFF_KI + IDX_DIM
A_IN = A_OFF_WI + IDX_HEADS

B_HEADS = 8
B_V_DIM = D_MODEL // B_HEADS
B_QK_DIM = B_V_DIM // 2
CHUNK = 64
B_OFF_K = B_HEADS * B_QK_DIM
B_OFF_V = 2 * B_HEADS * B_QK_DIM
B_OFF_O = B_OFF_V + B_HEADS * B_V_DIM
B_OFF_G = B_OFF_O + B_HEADS * B_V_DIM
B_IN = B_OFF_G + 2 * B_HEADS
M_INIT = -1e30

D_FF = 5632
CONV_WIDTH = 3

kernel_name = "hybrid_dsa_mlstm_convffn"

def rmsnorm(x, gain):
    xf = x.astype(jnp.float32)
    y = xf * lax.rsqrt(jnp.mean(xf * xf, axis=-1, keepdims=True) + EPS)
    return (y * gain.astype(jnp.float32)).astype(x.dtype)

def rope_tables(seq, dim):
    inv = 1.0 / (ROPE_THETA ** (jnp.arange(0, dim, 2, dtype=jnp.float32) / dim))
    ang = jnp.arange(seq, dtype=jnp.float32)[:, None] * inv[None, :]
    return jnp.cos(ang), jnp.sin(ang)

def apply_rope(x, cos, sin):
    xf = x.astype(jnp.float32)
    half = xf.shape[-1] // 2
    x1, x2 = xf[..., :half], xf[..., half:]
    c = cos[None, :, None, :]
    s = sin[None, :, None, :]
    return jnp.concatenate([x1 * c - x2 * s, x1 * s + x2 * c], axis=-1).astype(x.dtype)

def dsa_mixer(h, w_in, q_gain, k_gain, idx_k_gain, w_out, cos_a, sin_a, cos_i, sin_i):
    bsz, seq, _ = h.shape
    proj = h @ w_in
    q = proj[..., :A_OFF_K].reshape(bsz, seq, A_HEADS, A_HEAD_DIM)
    k = proj[..., A_OFF_K:A_OFF_V].reshape(bsz, seq, 1, A_HEAD_DIM)
    v = proj[..., A_OFF_V:A_OFF_QI]
    qi = proj[..., A_OFF_QI:A_OFF_KI].reshape(bsz, seq, IDX_HEADS, IDX_DIM)
    ki = proj[..., A_OFF_KI:A_OFF_WI].reshape(bsz, seq, 1, IDX_DIM)
    wi = proj[..., A_OFF_WI:].astype(jnp.float32) * (IDX_HEADS ** -0.5 * IDX_DIM ** -0.5)
    q = apply_rope(rmsnorm(q, q_gain), cos_a, sin_a)
    k = apply_rope(rmsnorm(k, k_gain), cos_a, sin_a)[:, :, 0]
    qi = apply_rope(qi, cos_i, sin_i)
    ki = apply_rope(rmsnorm(ki, idx_k_gain), cos_i, sin_i)[:, :, 0]

    n_keep = min(TOPK_MAX, seq // 4)
    qb = min(Q_BLOCK, seq)
    nblk = seq // qb
    key_pos = jnp.arange(seq, dtype=jnp.int32)

    def blocks(t):
        return jnp.swapaxes(t.reshape(bsz, nblk, qb, *t.shape[2:]), 0, 1)

    def attend_block(args):
        q_blk, qi_blk, wi_blk, q_pos = args
        causal = key_pos[None, None, :] <= q_pos[None, :, None]
        rel = jax.nn.relu(jnp.einsum('bqhd,bsd->bqhs', qi_blk, ki))
        score = jnp.einsum('bqhs,bqh->bqs', rel, wi_blk).astype(jnp.float32)
        score = jnp.where(causal, score, -jnp.inf)
        _, sel = lax.top_k(score, n_keep)
        valid = sel <= q_pos[None, :, None]
        k_sel = jax.vmap(lambda kb, ib: kb[ib])(k, sel)
        v_sel = jax.vmap(lambda vb, ib: vb[ib])(v, sel)
        logits = jnp.einsum('bqhd,bqkd->bqhk', q_blk, k_sel).astype(jnp.float32) * (A_HEAD_DIM ** -0.5)
        logits = jnp.where(valid[:, :, None, :], logits, -jnp.inf)
        p = jax.nn.softmax(logits, axis=-1).astype(v.dtype)
        return jnp.einsum('bqhk,bqkd->bqhd', p, v_sel)

    out = lax.map(attend_block, (blocks(q), blocks(qi), blocks(wi), key_pos.reshape(nblk, qb)))
    out = jnp.swapaxes(out, 0, 1).reshape(bsz, seq, A_Q_WIDTH)
    return out @ w_out

def to_chunks(t, nc, cl):
    t = t.reshape(t.shape[0], nc, cl, *t.shape[2:])
    return jnp.swapaxes(jnp.swapaxes(t, 0, 1), 2, 3)

def mlstm_chunkwise(q, k, v, log_i, log_f):
    bsz, seq, nh, dk = q.shape
    dv = v.shape[-1]
    cl = min(CHUNK, seq)
    nc = seq // cl
    tril = jnp.tril(jnp.ones((cl, cl), dtype=bool))

    def step(carry, inp):
        c_mat, n_vec, m = carry
        qj, kj, vj, li, lf = inp
        b = jnp.cumsum(lf, axis=-1)
        a = b + m[..., None]
        dmat = b[..., :, None] - b[..., None, :] + li[..., None, :]
        dmat = jnp.where(tril, dmat, -jnp.inf)
        m_t = jnp.maximum(a, jnp.max(dmat, axis=-1))
        inter = jnp.exp(a - m_t)
        s = jnp.einsum('bhtd,bhsd->bhts', qj, kj) * jnp.exp(dmat - m_t[..., None])
        num = inter[..., None] * jnp.einsum('bhtd,bhdv->bhtv', qj, c_mat) + jnp.einsum('bhts,bhsv->bhtv', s, vj)
        den = inter * jnp.einsum('bhtd,bhd->bht', qj, n_vec) + jnp.sum(s, axis=-1)
        hj = num / jnp.maximum(jnp.abs(den), jnp.exp(-m_t))[..., None]
        b_end = b[..., -1]
        g = b_end[..., None] - b + li
        m_new = jnp.maximum(b_end + m, jnp.max(g, axis=-1))
        decay = jnp.exp(b_end + m - m_new)
        wts = jnp.exp(g - m_new[..., None])
        c_new = decay[..., None, None] * c_mat + jnp.einsum('bhs,bhsd,bhsv->bhdv', wts, kj, vj)
        n_new = decay[..., None] * n_vec + jnp.einsum('bhs,bhsd->bhd', wts, kj)
        return (c_new, n_new, m_new), hj

    init = (jnp.zeros((bsz, nh, dk, dv), jnp.float32),
            jnp.zeros((bsz, nh, dk), jnp.float32),
            jnp.full((bsz, nh), M_INIT, jnp.float32))
    xs = (to_chunks(q, nc, cl), to_chunks(k, nc, cl), to_chunks(v, nc, cl),
          to_chunks(log_i, nc, cl), to_chunks(log_f, nc, cl))
    _, hs = lax.scan(step, init, xs)
    hs = jnp.swapaxes(jnp.swapaxes(hs, 2, 3), 0, 1)
    return hs.reshape(bsz, seq, nh, dv)

def mlstm_mixer(h, w_in, gate_bias, head_gain, w_out):
    bsz, seq, _ = h.shape
    proj = h @ w_in
    f32 = jnp.float32
    q = proj[..., :B_OFF_K].reshape(bsz, seq, B_HEADS, B_QK_DIM).astype(f32)
    k = proj[..., B_OFF_K:B_OFF_V].reshape(bsz, seq, B_HEADS, B_QK_DIM).astype(f32) * (B_QK_DIM ** -0.5)
    v = proj[..., B_OFF_V:B_OFF_O].reshape(bsz, seq, B_HEADS, B_V_DIM).astype(f32)
    o = jax.nn.sigmoid(proj[..., B_OFF_O:B_OFF_G].astype(f32))
    gates = proj[..., B_OFF_G:].astype(f32) + gate_bias.astype(f32)
    log_i = gates[..., :B_HEADS]
    log_f = jax.nn.log_sigmoid(gates[..., B_HEADS:])
    h_tilde = mlstm_chunkwise(q, k, v, log_i, log_f)
    h_norm = rmsnorm(h_tilde, head_gain.reshape(B_HEADS, B_V_DIM))
    h_out = (h_norm.reshape(bsz, seq, B_HEADS * B_V_DIM) * o).astype(h.dtype)
    return h_out @ w_out

def conv_ffn(h, w_up, conv_w, conv_b, w_down):
    up = h @ w_up
    gate, val = up[..., :D_FF], up[..., D_FF:]
    gate = lax.conv_general_dilated(
        gate, conv_w[:, None, :].astype(gate.dtype), window_strides=(1,),
        padding=[(CONV_WIDTH - 1, 0)], dimension_numbers=('NWC', 'WIO', 'NWC'),
        feature_group_count=D_FF) + conv_b
    return (jax.nn.gelu(gate, approximate=False) * val) @ w_down

def setup_inputs(seed: int = 0) -> dict:
    key = jax.random.key(seed)
    ks = jax.random.split(key, 20)

    def nrm(k, shape, scale):
        return jax.random.normal(k, shape, jnp.float32) * scale

    x = nrm(ks[0], (BATCH, SEQ, D_MODEL), 1.0)
    a_norm = 1.0 + nrm(ks[1], (N_A, D_MODEL), 0.02)
    a_w_in = nrm(ks[2], (N_A, D_MODEL, A_IN), D_MODEL ** -0.5)
    a_q_gain = 1.0 + nrm(ks[3], (N_A, A_HEAD_DIM), 0.02)
    a_k_gain = 1.0 + nrm(ks[4], (N_A, A_HEAD_DIM), 0.02)
    a_idx_k_gain = 1.0 + nrm(ks[5], (N_A, IDX_DIM), 0.02)
    a_w_out = nrm(ks[6], (N_A, A_Q_WIDTH, D_MODEL), A_Q_WIDTH ** -0.5)
    b_norm = 1.0 + nrm(ks[7], (N_B, D_MODEL), 0.02)
    b_w_in = nrm(ks[8], (N_B, D_MODEL, B_IN), D_MODEL ** -0.5)
    b_gate_bias = jnp.concatenate([nrm(ks[9], (N_B, B_HEADS), 0.1),
                                   3.0 + nrm(ks[10], (N_B, B_HEADS), 0.1)], axis=-1)
    b_head_norm = 1.0 + nrm(ks[11], (N_B, B_HEADS * B_V_DIM), 0.02)
    b_w_out = nrm(ks[12], (N_B, B_HEADS * B_V_DIM, D_MODEL), (B_HEADS * B_V_DIM) ** -0.5)
    f_norm = 1.0 + nrm(ks[13], (DEPTH, D_MODEL), 0.02)
    f_w_up = nrm(ks[14], (DEPTH, D_MODEL, 2 * D_FF), D_MODEL ** -0.5)
    f_conv_w = nrm(ks[15], (DEPTH, CONV_WIDTH, D_FF), CONV_WIDTH ** -0.5)
    f_conv_b = nrm(ks[16], (DEPTH, D_FF), 0.02)
    f_w_down = nrm(ks[17], (DEPTH, D_FF, D_MODEL), D_FF ** -0.5)
    return {"x": x, "a_norm": a_norm, "a_w_in": a_w_in, "a_q_gain": a_q_gain,
            "a_k_gain": a_k_gain, "a_idx_k_gain": a_idx_k_gain, "a_w_out": a_w_out,
            "b_norm": b_norm, "b_w_in": b_w_in, "b_gate_bias": b_gate_bias,
            "b_head_norm": b_head_norm, "b_w_out": b_w_out,
            "f_norm": f_norm, "f_w_up": f_w_up, "f_conv_w": f_conv_w,
            "f_conv_b": f_conv_b, "f_w_down": f_w_down}

def reference(x, a_norm, a_w_in, a_q_gain, a_k_gain, a_idx_k_gain, a_w_out,
              b_norm, b_w_in, b_gate_bias, b_head_norm, b_w_out,
              f_norm, f_w_up, f_conv_w, f_conv_b, f_w_down):
    seq = x.shape[1]
    cos_a, sin_a = rope_tables(seq, A_HEAD_DIM)
    cos_i, sin_i = rope_tables(seq, IDX_DIM)
    h = x
    for i in range(DEPTH):
        j = i // N_MIXERS
        if i % N_MIXERS == 0:
            h = h + dsa_mixer(rmsnorm(h, a_norm[j]), a_w_in[j], a_q_gain[j], a_k_gain[j],
                              a_idx_k_gain[j], a_w_out[j], cos_a, sin_a, cos_i, sin_i)
        else:
            h = h + mlstm_mixer(rmsnorm(h, b_norm[j]), b_w_in[j], b_gate_bias[j],
                                b_head_norm[j], b_w_out[j])
        h = h + conv_ffn(rmsnorm(h, f_norm[i]), f_w_up[i], f_conv_w[i], f_conv_b[i], f_w_down[i])
    return h


_drawn_inputs = setup_inputs


def setup_inputs(seed=0):
    import zlib

    import numpy as np

    out = dict(_drawn_inputs(seed))
    spreads = {}
    factors = {'a_q_gain': 8.0, 'a_k_gain': 8.0, 'b_norm': 2.98, 'b_head_norm': 6.492, 'f_conv_b': 3.277}
    for name, (base, spread) in spreads.items():
        noise = np.random.default_rng([zlib.crc32(name.encode()), seed]).standard_normal(out[name].shape)
        drawn = base * np.exp(spread * noise) if base else spread * noise
        out[name] = __import__('jax').numpy.asarray(drawn.astype(out[name].dtype))
    for name, factor in factors.items():
        out[name] = (out[name] * factor).astype(out[name].dtype)
    return out
```

```python
from contextlib import ExitStack

import concourse.bass as bass
from concourse import mybir

ALU = mybir.AluOpType
ACT = mybir.ActivationFunctionType
F32 = mybir.dt.float32
F32R = mybir.dt.float32r
AX_X = mybir.AxisListType.X

P = 128
D = 2048
T = 256
KT = D // P
NT = D // P
EPS = 1e-6
FF = 5632
HALF = FF // P // 2
QRT = HALF // 2
A_HEADS = 16
IDX_HEADS = 16
IDX_SCALE = IDX_HEADS ** -0.5 * 64 ** -0.5
N_KEEP = 64
B_HEADS = 8
LAYERS = 2

A_N = 4 + IDX_HEADS // 2 + A_HEADS
UP_N = 2 * HALF
DN_N = 2 * NT
B_N = 1 + 6 * B_HEADS
FFN_N = 2 * (UP_N + DN_N)
U_A = 0
U_OA = U_A + A_N
U_F0 = U_OA + NT
U_B = U_F0 + FFN_N
U_OB = U_B + B_N
U_F1 = U_OB + NT
U_F = [U_F0, U_F1]

X_A = 0
X_OA = X_A + KT
X_F0 = X_OA + A_HEADS
X_B = X_F0 + NT + 2 * HALF
X_OB = X_B + NT
X_F1 = X_OB + NT
X_F = [X_F0, X_F1]

C_F0 = A_N
C_B = C_F0 + 2 * UP_N
C_F1 = C_B + B_N
C_F = [C_F0, C_F1]

PIECES = [(0, 4, 1), (4, 8, 1), (8, 12, 1), (12, 16, 1)]
PIECES_DN = [(0, 4, 1), (4, 8, 1), (8, QRT, 2)]

MASKED = -3.0e38
PICKED = -3.39e38
PICKED_TEST = -3.38e38
NEG = -1e30

ROT, LOG, TRN, VAL = 4, 5, 6, 7


class Index:

    def __init__(self, turn, mult, add):
        self.turn, self.mult, self.add = turn, mult, add

    def __add__(self, n):
        return Index(self.turn, self.mult, self.add + n)

    def __sub__(self, n):
        return Index(self.turn, self.mult, self.add - n)

    def __mul__(self, n):
        return Index(self.turn, self.mult * n, self.add * n)

    def __floordiv__(self, n):
        assert self.mult % n == 0
        return Index(self.turn, self.mult // n, self.add // n)

    __radd__, __rmul__ = __add__, __mul__

    def value(self):
        scaled = self.turn * self.mult if self.mult > 1 else self.turn
        return scaled + self.add if self.add else scaled


def num(n):
    return n if isinstance(n, int) else n.value()


def exists(n, count):
    return not isinstance(n, int) or 0 <= n < count


def early(n, first):
    return isinstance(n, int) and n < first


def tile(t, n):
    return t[:, n, :] if isinstance(n, int) else t[:, bass.ds(num(n), 1), :].rearrange("p n t -> p (n t)")


def part(t, n, w):
    if isinstance(n, int):
        return t[:, n, w, :]
    return t[:, bass.ds(num(n), 1), w, :].rearrange("p n t -> p (n t)")


def scalar(t, n, *more):
    if isinstance(n, int):
        n = slice(n, n + 1)
    else:
        n = bass.ds(num(n), 1)
    if more:
        return t[:, n, more[0]:more[0] + 1].rearrange("p n m -> p (n m)")
    return t[:, n]


class Count:

    def __init__(self, eng, sem):
        self.eng, self.sem, self.done, self.shift = eng, sem, 0, 0

    def step(self, ins):
        self.done += 1
        ins.then_inc(self.sem, 1)

    def wait(self):
        self.eng.wait_ge(self.sem, num(self.shift + self.done))

    def enter(self, turn, per):
        self.first, self.per, self.shift = self.done, per, Index(turn, per, 0)

    def leave(self, turns):
        assert self.done - self.first == self.per, f"{self.done - self.first} steps in the loop, not {self.per}"
        self.done, self.shift = self.first + turns * self.per, 0


def loop(eng, start, stop, size, step, count=None, per=0):
    turns = (stop - start) // size
    assert turns * size == stop - start
    with eng.Fori(0, turns) as turn:
        if count:
            count.enter(turn, per)
        for j in range(size):
            step(Index(turn, size, start + j), start + j)
    if count:
        count.leave(turns)


def build(nc, xT, a_units, a_out, b_units, b_out, f_up, f_down, consts, tables, cols, norms, conv,
          gate_bias, out):
    with ExitStack() as ctx:
        def sb(name, shape, dt=F32):
            return ctx.enter_context(nc.sbuf_tensor(name, shape, dt))

        def sem(name):
            return ctx.enter_context(nc.semaphore(name))

        hT = sb("hT", [P, NT, T])
        xs = sb("xs", [P, KT, 2, T], F32R)
        mid = sb("mid", [P, HALF, 2, T], F32R)
        raw = sb("raw", [P, 4, KT * P])
        whi = sb("whi", [P, 2, KT * P], F32R)
        wlo = sb("wlo", [P, 2, KT * P], F32R)
        con = sb("con", [P, 4 * P])
        col = sb("col", [P, 6])
        nrm = sb("nrm", [P, 5, NT])
        cnv = sb("cnv", [P, LAYERS, 2 * HALF, 4])
        gbias = sb("gbias", [64, 1])
        cross = sb("cross", [P, 2, T])
        rB = sb("rB", [P, T])
        acc = sb("acc", [P, T])
        sqp = sb("sqp", [P, T])
        y = sb("y", [P, 2, T])
        ysq = sb("ysq", [P, 2, T])
        qT = sb("qT", [P, 2, T])
        kb = sb("kb", [P, 2, T])
        vT = sb("vT", [P, 2, T])
        hn = sb("hn", [P, 2, T])
        big = sb("big", [P, 2, 3 * P])
        sm = sb("sm", [P, 2, 8, 2])
        scr = sb("scr", [P, 24 * T])

        ident, rot_a, rot_i, ones = (con[:, n * P:(n + 1) * P] for n in range(4))

        def scratch(first, size):
            return scr[:, first * T:first * T + size]

        trig = scratch(0, 4 * T).rearrange("p (n t) -> p n t", n=4)
        tab = scratch(4, 6 * T).rearrange("p (n t) -> p n t", n=6)
        CQ, SQ, CK, SK, CKI, SKI = (tab[:, n, :] for n in range(6))
        kT = scratch(10, T)
        kiT = scratch(11, T)
        vN = scratch(12, T).rearrange("p (s d) -> p s d", s=2)
        rp = scratch(13, 2 * T).rearrange("p (n t) -> p n t", n=2)
        score = scratch(15, 3 * P)
        mbias = scr[:, 15 * T + 3 * P:18 * T]
        lg = scratch(18, 3 * P)
        pT = scr[:, 18 * T + 3 * P:21 * T]
        pp = scratch(21, 6 * P).rearrange("p (n t) -> p n t", n=2)
        QBLK = ((0, P), (P, 3 * P))
        wiN = sb("wiN", [P, 2, IDX_HEADS])
        mx8 = sb("mx8", [P, 8])
        mbb = scratch(0, 16 * T).rearrange("p (h n t) -> p h n t", h=B_HEADS, n=2)
        vN2 = scratch(16, 2 * T).rearrange("p (s v) -> p s v", s=2)
        so = scratch(18, 2 * T).rearrange("p (n t) -> p n t", n=2)
        mrow = scr[0:B_HEADS, 20 * T:22 * T]
        bt = scratch(22, 2 * T).rearrange("p (n t) -> p n t", n=2)
        aN = sb("aN", [P, 2, B_HEADS])
        fg = scratch(0, T + 2)
        fc = scratch(2, T)
        fgl = scratch(3, T)
        fv = scratch(4, 2 * T).rearrange("p (n t) -> p n t", n=2)

        bank = ctx.enter_context(nc.psum_tensor("bank", [P, 8, 2 * T], F32))

        s_raw = [sem(f"raw_loaded{n}") for n in range(4)]
        s_con = sem("constants_loaded")
        s_h0 = [sem(f"x_loaded{n}") for n in range(4)]
        s_hi = sem("weight_hi_ready")
        s_lo = sem("weight_lo_ready")
        s_mm = sem("pieces_multiplied")
        s_cross = sem("cross_copied")
        s_evac = sem("bank_read")
        s_xhi = sem("x_hi_ready")
        s_x = sem("x_ready")
        s_h = sem("h_tile_ready")
        s_acc = sem("squares_summed")
        s_nsum = sem("norm_sum_ready")
        s_nx = sem("norm_mean_ready")
        s_nr = sem("norm_guess_ready")
        s_act = sem("act_steps")
        s_dve = sem("dve_steps")
        s_pool = sem("pool_steps")
        s_clear = sem("pool_cleared")
        s_fc = sem("conv_ready")
        s_fgl = sem("gelu_ready")
        s_fh = sem("gelu_value_ready")
        s_y = sem("projection_ready")
        s_vy = sem("v_wi_ready")
        s_sq = sem("projection_squared")
        s_rot = sem("projection_rotated")
        s_kx = sem("key_mean_ready")
        s_kr = sem("key_guess_ready")
        s_krot = sem("key_rotation_read")
        s_kT = sem("key_ready")
        s_nat = sem("natural_ready")
        s_natc = sem("natural_copied")
        s_qi = sem("index_query_ready")
        s_isc = sem("index_products")
        s_rl = sem("index_relu")
        s_icomb = sem("index_scores_added")
        s_caus = sem("scores_causal")
        s_pick = sem("keys_picked")
        s_mask = sem("mask_ready")
        s_ms = sem("query_mean_ready")
        s_qT = sem("query_ready")
        s_r0 = sem("query_guess_ready")
        s_log = sem("logits_ready")
        s_nb = sem("softmax_bias_ready")
        s_ex = sem("exp_ready")
        s_pn = sem("probs_ready")
        s_pt = sem("probs_transposed")
        s_ptc = sem("probs_copied")
        s_o = sem("attention_out")
        s_gd = sem("gates_dve")
        s_ga = sem("gates_act")
        s_gt = sem("gates_transposed")
        s_bc = sem("m_broadcast")
        s_bcc = sem("m_broadcast_copied")
        s_bq = sem("mlstm_q_ready")
        s_bk = sem("mlstm_k_ready")
        s_bv = sem("mlstm_v_ready")
        s_bvt = sem("mlstm_v_transposed")
        s_bvn = sem("mlstm_v_natural")
        s_bo = sem("mlstm_o_ready")
        s_boe = sem("mlstm_o_exp")
        s_bS = sem("mlstm_products")
        s_bE = sem("mlstm_decay")
        s_bEm = sem("mlstm_decay_causal")
        s_bP = sem("mlstm_weights")
        s_bnum = sem("mlstm_num_den")
        s_bh = sem("mlstm_h")
        s_bsq = sem("mlstm_h_squared")
        s_bss = sem("mlstm_square_sum")
        s_bx = sem("mlstm_mean")
        s_br = sem("mlstm_guess")
        s_by = sem("mlstm_out")
        s_out = sem("output_stored")

        block = ctx.enter_context(nc.Block())

        @block.sync
        def _(sp):
            def load(src, U, k, width=KT * P):
                if not early(U, 4):
                    sp.wait_ge(s_lo, num((U - 3) * 4))
                sp.dma_start(raw[:, k % 4, 0:width], src).then_inc(s_raw[k % 4], 16)

            def load_x(n):
                sp.dma_start(hT[:, 4 * n:4 * n + 4, :],
                             xT[4 * n * P:4 * (n + 1) * P, :].rearrange("(k p) t -> p k t", p=P)).then_inc(s_h0[n], 16)

            for dst, src in ((nrm, norms), (con, consts), (scr[:, 0:4 * T], tables), (col, cols),
                             (cnv, conv), (gbias, gate_bias)):
                if dst is nrm:
                    sp.dma_start(dst[:], src).then_inc(s_con, 16)
                    load_x(0)
                    load(a_units[0], 0, 0)
                    for n in range(1, 4):
                        load_x(n)
                    for n in range(1, 4):
                        load(a_units[n], n, n)
                else:
                    sp.dma_start(dst if dst.shape[1] == 4 * T else dst[:], src).then_inc(s_con, 16)

            def stream(src, U0, n, width=KT * P, first=0):
                odd = (n - first) % 4
                for j in range(first, first + odd):
                    load(src[j], U0 + j, U0 + j, width)
                first += odd
                loop(sp, first, n, 4, lambda i, k: load(
                    src[bass.ds(num(i), 1)].rearrange("a p n -> (a p) n"), U0 + i, U0 + k, width))

            stream(a_units, U_A, A_N, first=4)
            stream(a_out, U_OA, NT)
            for layer in range(LAYERS):
                for half in range(2):
                    U = U_F[layer] + half * (UP_N + DN_N)
                    stream(f_up[layer, half], U, UP_N)
                    stream(f_down[layer, half], U + UP_N, DN_N, QRT * P)
                if layer == 0:
                    stream(b_units, U_B, B_N)
                    stream(b_out, U_OB, NT)
            for n in range(4):
                sp.wait_ge(s_h, num(3 * NT + 4 * (n + 1)))
                sp.dma_start(out[4 * n * P:4 * (n + 1) * P, :].rearrange("(k p) t -> p k t", p=P),
                             hT[:, 4 * n:4 * n + 4, :]).then_inc(s_out, 16)
            sp.wait_ge(s_out, 64)

        @block.gpsimd
        def _(pool):
            c = Count(pool, s_pool)

            def clear():
                c.step(nc.gpsimd.memset(acc[:], 0.0))
                c.wait()

            def add_square(n):
                c.step(nc.gpsimd.tensor_tensor(sqp[:], tile(hT, n), tile(hT, n), ALU.mult))
                c.wait()
                c.step(nc.gpsimd.tensor_tensor(acc[:], acc[:], sqp[:], ALU.add))
                c.wait()

            def sum_squares(norm):
                pool.wait_ge(s_nsum, num(norm))
                clear()

                def one(n, k):
                    pool.wait_ge(s_h, num((norm - 1) * NT + 1 + n))
                    add_square(n)
                loop(pool, 0, NT, 4, one, c, 8)
                c.step(nc.gpsimd.tensor_copy(sqp[:, 0:1], acc[:, 0:1]))
                c.wait()
                nc.gpsimd.tensor_copy(sqp[:, 1:2], acc[:, 1:2]).then_inc(s_acc, 1)

            clear()
            for n in range(NT):
                if n % 4 == 0:
                    pool.wait_ge(s_h0[n // 4], 16)
                add_square(n)
            nc.gpsimd.memset(score, 0.0).then_inc(s_acc, 1)

            pool.wait_ge(s_icomb, num(IDX_HEADS // 2))
            for d in (0, 2):
                blk = score[:, d * P:(d + 1) * P]
                nc.gpsimd.affine_select(out=blk, in_=blk, compare_op=ALU.is_ge, fill=MASKED, base=0,
                                        pattern=[[-1, P]], channel_multiplier=1).then_inc(s_caus, 1)
            pool.wait_ge(s_pick, 1)
            for d in (0, 2):
                blk = mbias[:, d * P:(d + 1) * P]
                nc.gpsimd.affine_select(out=blk, in_=blk, compare_op=ALU.is_ge, fill=NEG, base=0,
                                        pattern=[[-1, P]], channel_multiplier=1).then_inc(s_mask, 1)
            sum_squares(1)
            pool.wait_ge(s_h, num(NT))
            nc.gpsimd.memset(fg[:, 0:2], 0.0).then_inc(s_clear, 1)
            sum_squares(2)

            for h in range(B_HEADS):
                pool.wait_ge(s_bE, h + 1)
                for d in (0, 2):
                    blk = big[:, h % 2, d * P:(d + 1) * P]
                    nc.gpsimd.affine_select(out=blk, in_=blk, compare_op=ALU.is_ge, fill=0.0, base=0,
                                            pattern=[[1, P]], channel_multiplier=-1).then_inc(s_bEm, 1)
            sum_squares(3)
            nc.gpsimd.memset(fg[:, 0:2], 0.0).then_inc(s_clear, 1)

        @block.scalar
        def _(act):
            c = Count(act, s_act)

            def split(U, k, pieces=PIECES):
                act.wait_ge(s_raw[k % 4], num((U - k % 4) * 4 + 16))
                for p, (a, z, inc) in enumerate(pieces):
                    if not early(U, 2):
                        act.wait_ge(s_mm, num((U - 2) * 4 + (p + 1)))
                    nc.scalar.activation(whi[:, k % 2, a * P:z * P], raw[:, k % 4, a * P:z * P],
                                         ACT.Copy).then_inc(s_hi, inc)

            def copy_cross(U, k, i, C):
                act.wait_ge(s_mm, num((U + 1) * 4))
                if not early(i, 2):
                    act.wait_ge(s_evac, num(U - 1))
                nc.scalar.activation(cross[:, C % 2, :], bank[:, k % 4, T:2 * T],
                                     ACT.Copy).then_inc(s_cross, 1)

            def x_hi(n, norm, sem, value):
                act.wait_ge(sem, num(value))
                nc.scalar.activation(part(xs, n, 0), tile(hT, n), ACT.Copy,
                                     scale=scalar(nrm[:, norm, :], n)).then_inc(s_xhi, 1)

            def guess(dst, tmp, src, done):
                c.step(nc.scalar.activation(tmp, src, ACT.Ln))
                c.wait()
                nc.scalar.activation(dst, tmp, ACT.Exp, scale=-0.5).then_inc(done, 1)

            def norm_guess(norm):
                act.wait_ge(s_nx, num(norm + 1))
                guess(kb[:, 0, :], hn[:, 1, :], hn[:, 0, :], s_nr)

            def a_step(i, k):
                if i == 2:
                    norm_guess(0)
                if exists(i - 2, A_N):
                    copy_cross(i - 2 + U_A, k - 2 + U_A, i - 2, k - 2)
                if i == 2 or i == 3:
                    act.wait_ge(s_y, num(i - 1))
                    nc.scalar.activation(ysq[:, i - 2, :], y[:, i - 2, :], ACT.Square).then_inc(s_sq, 1)
                if i == 4 or i == 5:
                    act.wait_ge(s_kx, num(i - 3))
                    guess(kb[:, i - 4, :], hn[:, i - 4, :], big[:, i - 4, 0:T], s_kr)
                if i == 5:
                    act.wait_ge(s_nat, 1)
                    nc.scalar.activation(vN[:], bank[:, TRN, 0:T].rearrange("p (s d) -> p s d", s=2),
                                         ACT.Copy).then_inc(s_natc, 1)
                if i == 6:
                    act.wait_ge(s_nat, 2)
                    nc.scalar.activation(
                        wiN[:], bank[:, TRN, T:T + 2 * IDX_HEADS].rearrange("p (s d) -> p s d", s=2),
                        ACT.Copy).then_inc(s_natc, 1)
                if isinstance(i, int) and 8 <= i < 16:
                    t = i - 8
                    for m in range(2):
                        act.wait_ge(s_isc, num(2 * t + m + 1))
                        if t and m == 0:
                            act.wait_ge(s_icomb, num(t))
                        nc.scalar.activation(big[:, m, :], bank[:, LOG + m, 0:3 * P],
                                             ACT.Relu).then_inc(s_rl, 1)
                h, j = i - 14, k - 14
                if exists(h, A_HEADS):
                    act.wait_ge(s_y, num(h + 11))
                    nc.scalar.activation(ysq[:, j % 2, :], y[:, j % 2, :], ACT.Square).then_inc(s_sq, 1)
                if exists(h - 1, A_HEADS):
                    act.wait_ge(s_ms, num(h))
                    m = sm[:, (j - 1) % 2]
                    guess(m[:, 2, :], m[:, 1, :], m[:, 0, :], s_r0)
                if exists(h - 5, A_HEADS):
                    act.wait_ge(s_o, num(h - 4))
                    nc.scalar.activation(part(mid, h - 5, 0), bank[:, VAL, 0:T], ACT.Copy).then_inc(s_xhi, 1)
                if exists(h - 4, A_HEADS):
                    act.wait_ge(s_pt, num(h - 3))
                    nc.scalar.activation(pT[:], bank[:, TRN, 0:3 * P], ACT.Copy).then_inc(s_ptc, 1)
                if exists(h - 2, A_HEADS):
                    act.wait_ge(s_nb, num(h - 1))
                    if not early(h - 2, 2):
                        act.wait_ge(s_pt, num(h - 3))
                    m = sm[:, j % 2]
                    for q, (a, z) in enumerate(QBLK):
                        nc.scalar.activation(pp[:, j % 2, a:z], lg[:, a:z], ACT.Exp, bias=m[:, 4, q:q + 1],
                                             scale=m[:, 3, q:q + 1],
                                             accum_out=m[:, 5, q:q + 1]).then_inc(s_ex, 1)

            def out_step(i, k, layer):
                if exists(i - 3, NT):
                    x_hi(i - 3, 2 * layer + 1, s_h, 2 * layer * NT + (i - 2))

            def up_step(i, k, layer, half):
                U0, C0 = U_F[layer] + half * (UP_N + DN_N), C_F[layer] + half * UP_N
                tiles = (2 * layer + half) * HALF
                if exists(i - 2, UP_N):
                    copy_cross(U0 + i - 2, U0 + k - 2, i - 2, C0 + k - 2)
                if k % 2 == 1:
                    f = (i - 3) // 2
                    if exists(f, HALF):
                        act.wait_ge(s_fc, num(tiles + 1 + f))
                        if not early(f, 1):
                            act.wait_ge(s_fh, num(tiles + f))
                        nc.scalar.activation(fgl[:], fc[:], ACT.Gelu).then_inc(s_fgl, 1)
                else:
                    f = (i - 4) // 2
                    if exists(f, HALF):
                        act.wait_ge(s_fh, num(tiles + 1 + f))
                        nc.scalar.activation(part(mid, f, 0), fv[:, 1, :], ACT.Copy).then_inc(s_xhi, 1)

            def down_step(i, k, layer, half):
                if half and k % 2 == 0 and layer < LAYERS - 1:
                    n = (i - 4) // 2
                    if exists(n, NT):
                        x_hi(n, 2 * layer + 2, s_h, (2 * layer + 1) * NT + 1 + n)

            def b_step(i, k):
                if exists(i - 2, B_N):
                    copy_cross(U_B + i - 2, U_B + k - 2, i - 2, C_B + k - 2)
                if i == 2:
                    act.wait_ge(s_gd, 1)
                    c.step(nc.scalar.activation(ysq[0:B_HEADS, 1, :], ysq[0:B_HEADS, 0, :], ACT.Exp, scale=-1.0))
                    c.wait()
                    nc.scalar.activation(big[0:B_HEADS, 0, 0:T], ysq[0:B_HEADS, 1, :], ACT.Ln,
                                         bias=1.0).then_inc(s_ga, 1)
                if i == 3:
                    act.wait_ge(s_gd, 3)
                    nc.scalar.activation(mrow[:, T:2 * T], hn[0:B_HEADS, 1, :], ACT.Exp,
                                         scale=-1.0).then_inc(s_ga, 1)
                if i == 4:
                    act.wait_ge(s_gt, 1)
                    nc.scalar.activation(aN[:], bank[:, TRN, 0:2 * B_HEADS].rearrange("p (s h) -> p s h", s=2),
                                         ACT.Copy).then_inc(s_ga, 1)
                for pair, when in enumerate((5, 6, 7, 7)):
                    if isinstance(i, int) and i == when:
                        for m in range(2):
                            act.wait_ge(s_bc, num(2 * pair + m + 1))
                            nc.scalar.activation(mbb[:, 2 * pair + m].rearrange("p n t -> p (n t)"),
                                                 bank[:, (ROT, VAL)[m], :], ACT.Copy).then_inc(s_bcc, 1)
                r = (k - 1) % 6
                h, j = (i - 1) // 6, (k - 1) // 6
                g, l = h - 1, j - 1
                if r == 0 and exists(g, B_HEADS):
                    natural(g, 1)
                if r == 1 and exists(g, B_HEADS):
                    exp_o(g, 0)
                    act.wait_ge(s_bh, num(g + 1))
                    nc.scalar.activation(ysq[:], hn[:], ACT.Square).then_inc(s_bsq, 1)
                if r == 2 and exists(g, B_HEADS):
                    exp_o(g, 1)
                    act.wait_ge(s_bx, num(g + 1))
                    guess(big[:, l % 2, 0:T], vT_tmp, bt[:, 0, :], s_br)
                if r == 4 and exists(g, B_HEADS):
                    for m in range(2):
                        act.wait_ge(s_by, num(g * 2 + (m + 1)))
                        nc.scalar.activation(part(mid, g * 2 + m, 0), y[:, m, :], ACT.Copy).then_inc(s_xhi, 1)
                if r == 4 and exists(h, B_HEADS):
                    if early(h, 2):
                        act.wait_ge(s_ga, 3)
                        act.wait_ge(s_bcc, (2, B_HEADS)[h])
                    for q, (a, z, t0) in enumerate(((0, 2 * P, 0), (2 * P, 3 * P, P))):
                        ins = nc.scalar.activation(big[:, j % 2, a:z], part(mbb, h, 0)[:, t0:T], ACT.Exp,
                                                   scale=-1.0, bias=scalar(aN[:, q, :], h))
                        if q == 0:
                            c.step(ins)
                    ins.then_inc(s_bE, 1)
                if r == 5 and exists(h, B_HEADS):
                    natural(h, 0)

            def natural(h, m):
                act.wait_ge(s_bvt, num(h * 2 + (m + 1)))
                nc.scalar.activation(vN2[:, :, m * P:(m + 1) * P],
                                     bank[:, (TRN, VAL)[m], 0:T].rearrange("p (s v) -> p s v", s=2),
                                     ACT.Copy).then_inc(s_bvn, 1)

            def exp_o(h, m):
                act.wait_ge(s_bo, num(h * 2 + (m + 1)))
                nc.scalar.activation(so[:, m, :], so[:, m, :], ACT.Exp, scale=-1.0).then_inc(s_boe, 1)

            vT_tmp = kb[:, 0, :]

            act.preload_act_table_set("natural_log_exp_and_others")
            act.wait_ge(s_con, 96)
            for n in range(KT):
                x_hi(n, 0, s_h0[n // 4], 16)

            for i in range(20):
                split(i, i)
                a_step(i, i)

            def a_turn(i, k):
                split(U_A + i, U_A + k)
                a_step(i, k)
            loop(act, 20, A_N, 4, a_turn, c, 4)

            def run_out(layer, U0, N_before, tail):
                def turn(i, k):
                    split(U0 + i, U0 + k)
                    out_step(i, k, layer)
                for i in range(4):
                    split(U0 + i, U0 + i)
                    tail(i)
                    out_step(i, i, layer)
                loop(act, 4, NT, 4, turn)

            def a_tail(i):
                for s in ((A_N,), range(A_N + 1, A_N + 7))[i] if i < 2 else ():
                    a_step(s, s)

            def b_tail(i):
                for s in ((B_N,), range(B_N + 1, B_N + 5))[i] if i < 2 else ():
                    b_step(s, s)

            def run_ffn(layer):
                for half in range(2):
                    U0 = U_F[layer] + half * (UP_N + DN_N)

                    def up(i, k):
                        split(U0 + i, U0 + k)
                        up_step(i, k, layer, half)
                    for i in range(4):
                        split(U0 + i, U0 + i)
                        if half == 0:
                            for s in ((NT,), (NT + 1, NT + 2))[i] if i < 2 else ():
                                out_step(s, s, layer)
                            if i == 2:
                                norm_guess(2 * layer + 1)
                        up_step(i, i, layer, half)
                    loop(act, 4, UP_N, 4, up)

                    U1 = U0 + UP_N

                    def down(i, k):
                        split(U1 + i, U1 + k, PIECES_DN)
                        down_step(i, k, layer, half)
                    for i in range(4):
                        split(U1 + i, U1 + i, PIECES_DN)
                        for s in ((UP_N,), (UP_N + 1, UP_N + 2))[i] if i < 2 else ():
                            up_step(s, s, layer, half)
                        down_step(i, i, layer, half)
                    loop(act, 4, DN_N, 4, down)

            run_out(0, U_OA, A_N, a_tail)
            run_ffn(0)
            act.preload_act_table_set("natural_log_exp_and_others")
            for i in range(13):
                split(U_B + i, U_B + i)
                for s in ((DN_N,), (DN_N + 1, DN_N + 2))[i] if i < 2 else ():
                    down_step(s, s, 0, 1)
                if i == 2:
                    norm_guess(2)
                b_step(i, i)

            def b_turn(i, k):
                split(U_B + i, U_B + k)
                b_step(i, k)
            loop(act, 13, B_N, 12, b_turn, c, 4)
            run_out(1, U_OB, B_N, b_tail)
            run_ffn(1)

        @block.vector
        def _(dve):
            c = Count(dve, s_dve)
            V = nc.vector

            def split(U, k, pieces=PIECES):
                for p, (a, z, inc) in enumerate(pieces):
                    dve.wait_ge(s_hi, num(U * 4 + (p + 1)))
                    V.tensor_tensor(wlo[:, k % 2, a * P:z * P], raw[:, k % 4, a * P:z * P],
                                    whi[:, k % 2, a * P:z * P].bitcast(F32), ALU.subtract).then_inc(s_lo, inc)

            def step(ins):
                c.step(ins)
                c.wait()

            def evac(U, k, C, k2, dst, done=None, factor=1.0):
                dve.wait_ge(s_cross, num(C + 1))
                V.tensor_tensor(dst, bank[:, k % 4, 0:T], cross[:, k2 % 2, :], ALU.add).then_inc(s_evac, 1)
                dve.wait_ge(s_evac, num(U + 1))
                ins = V.scalar_tensor_tensor(dst, dst, factor, rB[:], ALU.mult, ALU.mult)
                if done is None:
                    step(ins)
                else:
                    ins.then_inc(done, 1)

            def x_lo(n, norm, X):
                dve.wait_ge(s_xhi, num(X + 1 + n))
                V.scalar_tensor_tensor(part(xs, n, 1), tile(hT, n), scalar(nrm[:, norm, :], n),
                                       part(xs, n, 0).bitcast(F32), ALU.mult, ALU.subtract).then_inc(s_x, 1)

            def exact(x, r, tmp, dst, done=None, factor=1.0):
                step(V.tensor_tensor(tmp, r, r, ALU.mult))
                step(V.tensor_tensor(tmp, tmp, x, ALU.mult))
                step(V.tensor_scalar(tmp, tmp, -0.5 * factor, 1.5 * factor, ALU.mult, ALU.add))
                ins = V.tensor_tensor(dst, r, tmp, ALU.mult)
                if done is None:
                    step(ins)
                else:
                    ins.then_inc(done, 1)

            def mean(dst, src, n, done, extra=EPS):
                V.tensor_scalar(dst, src, 1.0 / n, extra, ALU.mult, ALU.add).then_inc(done, 1)

            def norm_factor(norm):
                dve.wait_ge(s_nsum, num(norm + 1))
                mean(hn[:, 0, :], bank[:, VAL, 0:T], D, s_nx)
                dve.wait_ge(s_nr, num(norm + 1))
                exact(hn[:, 0, :], kb[:, 0, :], kb[:, 1, :], rB[:])

            def rotate(src, cos, sin, dst, done, read=None):
                step(V.tensor_tensor(rp[:, 0, :], src, cos, ALU.mult))
                ins = V.tensor_tensor(rp[:, 1, :], bank[:, ROT, 0:T], sin, ALU.mult)
                if read is None:
                    step(ins)
                else:
                    ins.then_inc(read, 1)
                    dve.wait_ge(read, num(self_count[0]))
                ins = V.tensor_tensor(dst, rp[:, 0, :], rp[:, 1, :], ALU.add)
                if done is None:
                    step(ins)
                else:
                    ins.then_inc(done, 1)

            self_count = [0]

            def pick_keys():
                dve.wait_ge(s_caus, 2)
                for a, z in QBLK:
                    for _ in range(N_KEEP // 8):
                        step(V.max(mx8[:], score[:, a:z]))
                        step(V.match_replace(score[:, a:z], mx8[:], score[:, a:z], PICKED))
                V.tensor_scalar(mbias[:], score[:], PICKED_TEST, NEG, ALU.is_gt, ALU.mult).then_inc(s_pick, 1)
                dve.wait_ge(s_mask, 2)

            def a_step(i, k):
                if i == 2:
                    norm_factor(0)
                if i == 2 or i == 3:
                    evac(i - 2, i - 2, i - 2, i - 2, y[:, i - 2, :], s_y)
                if i == 3 or i == 4:
                    n = i - 3
                    dve.wait_ge(s_rot, num(n + 1))
                    mean(big[:, n, 0:T], bank[:, ROT, T:2 * T], P, s_kx)
                    self_count[0] = n + 1
                    rotate(y[:, n, :], (CKI, CK)[n], (SKI, SK)[n], (kiT, kT)[n], None, s_krot)
                if i == 4:
                    evac(2, 2, 2, 2, vT[:, 0, :], s_vy)
                if i == 4 or i == 5:
                    n = i - 4
                    dst = (kiT, kT)[n]
                    dve.wait_ge(s_kr, num(n + 1))
                    exact(big[:, n, 0:T], kb[:, n, :], hn[:, n, :], kb[:, n, :])
                    V.tensor_tensor(dst, dst, kb[:, n, :], ALU.mult).then_inc(s_kT, 1)
                if i == 5:
                    evac(3, 3, 3, 3, vT[:, 1, :], s_vy, factor=IDX_SCALE)
                if isinstance(i, int) and 6 <= i < 14:
                    evac(i - 2, i - 2, i - 2, i - 2, y[:, i % 2, :], s_y)
                if isinstance(i, int) and 7 <= i < 15:
                    t = i - 7
                    dve.wait_ge(s_rot, num(t + 3))
                    rotate(y[:, t % 2, :], trig[:, 2, :], trig[:, 3, :], qT[:, t % 2, :], s_qi)
                if isinstance(i, int) and 8 <= i < 16:
                    t = i - 8
                    if t == 0:
                        dve.wait_ge(s_natc, 2)
                        dve.wait_ge(s_acc, 1)
                    for m in range(2):
                        dve.wait_ge(s_rl, num(2 * t + m + 1))
                        for q, (a, z) in enumerate(QBLK):
                            ins = V.scalar_tensor_tensor(score[:, a:z], big[:, m, a:z],
                                                         wiN[:, q, 2 * t + m:2 * t + m + 1], score[:, a:z],
                                                         ALU.mult, ALU.add)
                            if m == 0 or q == 0:
                                step(ins)
                    ins.then_inc(s_icomb, 1)
                    dve.wait_ge(s_icomb, num(t + 1))
                if i == 16:
                    pick_keys()
                h, j = i - 14, k - 14
                if exists(h, A_HEADS):
                    evac(i - 2, k - 2, i - 2, k - 2, y[:, j % 2, :], s_y)
                if exists(h - 1, A_HEADS):
                    m = sm[:, (j - 1) % 2]
                    dve.wait_ge(s_rot, num(h + 10))
                    mean(m[:, 0, :], bank[:, ROT, T:T + 2], P, s_ms)
                    rotate(y[:, (j - 1) % 2, :], CQ, SQ, qT[:, (j - 1) % 2, :], s_qT)
                if exists(h - 2, A_HEADS):
                    m = sm[:, j % 2]
                    dve.wait_ge(s_r0, num(h - 1))
                    exact(m[:, 0, :], m[:, 2, :], m[:, 1, :], m[:, 3, :], factor=P ** -0.5)
                    dve.wait_ge(s_log, num(h - 1))
                    if not early(h - 2, 1):
                        dve.wait_ge(s_ex, num((h - 2) * 2))
                    V.memset(mx8[:, 0:1], 0.0)
                    for q, (a, z) in enumerate(QBLK):
                        c.step(V.tensor_tensor_reduce(lg[:, a:z], bank[:, LOG, a:z], mbias[:, a:z], 1.0, MASKED,
                                                      ALU.add, ALU.max, m[:, 6, q:q + 1]))
                    c.wait()
                    V.scalar_tensor_tensor(m[:, 4, :], m[:, 6, :], -1.0, m[:, 3, :], ALU.mult,
                                           ALU.mult).then_inc(s_nb, 1)
                if exists(h - 3, A_HEADS):
                    m = sm[:, (j - 1) % 2]
                    dve.wait_ge(s_ex, num((h - 2) * 2))
                    step(V.reciprocal(m[:, 7, :], m[:, 5, :]))
                    for q, (a, z) in enumerate(QBLK):
                        ins = V.tensor_scalar(pp[:, (j - 1) % 2, a:z], pp[:, (j - 1) % 2, a:z],
                                              m[:, 7, q:q + 1], None, ALU.mult)
                        if q == 0:
                            c.step(ins)
                    ins.then_inc(s_pn, 1)
                if exists(h - 5, A_HEADS):
                    dve.wait_ge(s_xhi, num(X_OA + (h - 4)))
                    V.tensor_tensor(part(mid, h - 5, 1), bank[:, VAL, 0:T], part(mid, h - 5, 0).bitcast(F32),
                                    ALU.subtract).then_inc(s_x, 1)

            def add_h(n, U_last, k, units, done):
                dve.wait_ge(s_mm, num((U_last + 1) * 4))
                step(V.tensor_tensor(tile(hT, n), tile(hT, n), bank[:, k % 4, 0:T], ALU.add))
                V.tensor_tensor(tile(hT, n), tile(hT, n), bank[:, k % 4, T:2 * T],
                                ALU.add).then_inc(s_evac, units)
                dve.wait_ge(s_evac, num(U_last + 1))
                if done:
                    dve.sem_inc(s_h, 1)

            def out_step(i, k, layer):
                U0 = (U_OA, U_OB)[layer]
                if exists(i - 2, NT):
                    add_h(i - 2, U0 + i - 2, U0 + k - 2, 1, True)
                if exists(i - 3, NT):
                    x_lo(i - 3, 2 * layer + 1, X_F[layer])

            def up_step(i, k, layer, half):
                U0, C0 = U_F[layer] + half * (UP_N + DN_N), C_F[layer] + half * UP_N
                tiles = (2 * layer + half) * HALF
                X0 = X_F[layer] + NT + half * HALF
                if k % 2 == 0:
                    f = (i - 4) // 2
                    if exists(f, HALF):
                        dve.wait_ge(s_xhi, num(X0 + 1 + f))
                        V.tensor_tensor(part(mid, f, 1), fv[:, 1, :], part(mid, f, 0).bitcast(F32),
                                        ALU.subtract).then_inc(s_x, 1)
                    f = (i - 2) // 2
                    if exists(f, HALF):
                        taps = [scalar(cnv[:, layer, :, m], f + half * HALF) for m in range(4)]
                        evac(U0 + i - 2, U0 + k - 2, C0 + i - 2, C0 + k - 2, fg[:, 2:T + 2])
                        step(V.tensor_scalar(fc[:], fg[:, 0:T], taps[0], taps[3], ALU.mult, ALU.add))
                        step(V.scalar_tensor_tensor(fc[:], fg[:, 1:T + 1], taps[1], fc[:], ALU.mult, ALU.add))
                        V.scalar_tensor_tensor(fc[:], fg[:, 2:T + 2], taps[2], fc[:], ALU.mult,
                                               ALU.add).then_inc(s_fc, 1)
                else:
                    f = (i - 3) // 2
                    if exists(f, HALF):
                        evac(U0 + i - 2, U0 + k - 2, C0 + i - 2, C0 + k - 2, fv[:, 0, :])
                        dve.wait_ge(s_fgl, num(tiles + 1 + f))
                        V.tensor_tensor(fv[:, 1, :], fv[:, 0, :], fgl[:], ALU.mult).then_inc(s_fh, 1)

            def down_step(i, k, layer, half):
                U0 = U_F[layer] + half * (UP_N + DN_N) + UP_N
                final = half == 1
                if k % 2 == 1:
                    n = (i - 3) // 2
                    if exists(n, NT):
                        add_h(n, U0 + i - 2, U0 + k - 3, 2, final)
                elif final and layer < LAYERS - 1:
                    n = (i - 4) // 2
                    if exists(n, NT):
                        x_lo(n, 2 * layer + 2, X_B)

            def gates():
                G = B_HEADS
                evac(U_B, U_B, C_B, C_B, y[:, 0, :])
                li, xf, ax, l1 = hn[0:G, 0, :], hn[0:G, 1, :], ysq[0:G, 0, :], big[0:G, 0, 0:T]
                lf, B, a, M = ysq[0:G, 1, :], kb[0:G, 0, :], kb[0:G, 1, :], mrow[:, 0:T]
                step(V.tensor_scalar(li, y[0:G, 0, :], gbias[0:G, :], None, ALU.add))
                step(V.tensor_scalar(xf, y[32:32 + G, 0, :], gbias[32:32 + G, :], None, ALU.add))
                V.scalar_tensor_tensor(ax, xf, -1.0, xf, ALU.mult, ALU.max).then_inc(s_gd, 1)
                step(V.memset(vT[0:G, 1, :], 1.0))
                dve.wait_ge(s_ga, 1)
                step(V.tensor_scalar(lf, xf, 0.0, None, ALU.min))
                step(V.tensor_tensor(lf, lf, l1, ALU.subtract))
                step(V.tensor_tensor_scan(B, vT[0:G, 1, :], lf, 0.0, ALU.mult, ALU.add))
                V.tensor_tensor(a, li, B, ALU.subtract).then_inc(s_gd, 1)
                dve.wait_ge(s_gd, 2)
                step(V.tensor_tensor_scan(M, a, a, MASKED, ALU.max, ALU.max))
                V.tensor_tensor(hn[0:G, 1, :], B, M, ALU.add).then_inc(s_gd, 1)

            def b_evac(i, k, dst, done, factor=1.0):
                evac(U_B + i - 2, U_B + k - 2, C_B + i - 2, C_B + k - 2, dst, done, factor)

            def b_step(i, k):
                if i == 2:
                    gates()
                r = (k - 1) % 6
                h, j = (i - 1) // 6, (k - 1) // 6
                g, l = h - 1, j - 1
                if r == 2 and exists(h, B_HEADS):
                    b_evac(i, k, qT[:, j % 2, :], s_bq)
                if r == 3 and exists(h, B_HEADS):
                    if early(h, 1):
                        dve.wait_ge(s_gt, 1)
                    b_evac(i, k, kb[:, 1, :], s_bk, P ** -0.5)
                if r == 4 and exists(h, B_HEADS):
                    b_evac(i, k, vT[:, 0, :], s_bv)
                if r == 5 and exists(h, B_HEADS):
                    b_evac(i, k, vT[:, 1, :], s_bv)
                    dve.wait_ge(s_bS, num(h + 1))
                    dve.wait_ge(s_bEm, num(h * 2 + 2))
                    V.tensor_tensor(big[:, j % 2, :], bank[:, LOG, 0:3 * P], big[:, j % 2, :],
                                    ALU.mult).then_inc(s_bP, 1)
                if r in (0, 1) and exists(g, B_HEADS):
                    b_evac(i, k, so[:, r, :], s_bo)
                if r == 1 and exists(g, B_HEADS):
                    dve.wait_ge(s_bnum, num(g + 1))
                    step(V.tensor_tensor(bt[:, 0, :], bank[:, ROT, 0:T], part(mbb, g, 1), ALU.max))
                    step(V.scalar_tensor_tensor(bt[:, 0, :], bank[:, ROT, 0:T], -1.0, bt[:, 0, :], ALU.mult, ALU.max))
                    step(V.reciprocal(bt[:, 1, :], bt[:, 0, :]))
                    for m in range(2):
                        ins = V.tensor_tensor(hn[:, m, :], bank[:, VAL, m * T:(m + 1) * T], bt[:, 1, :], ALU.mult)
                        if m == 0:
                            c.step(ins)
                    ins.then_inc(s_bh, 1)
                if r == 2 and exists(g, B_HEADS):
                    dve.wait_ge(s_bss, num(g + 1))
                    mean(bt[:, 0, :], bank[:, ROT, T:2 * T], 2 * P, s_bx)
                if r in (2, 3) and exists(g, B_HEADS):
                    m = r - 2
                    dve.wait_ge(s_boe, num(g * 2 + (m + 1)))
                    step(V.tensor_scalar(so[:, m, :], so[:, m, :], 1.0, None, ALU.add))
                    step(V.reciprocal(so[:, m, :], so[:, m, :]))
                if r == 3 and exists(g, B_HEADS):
                    dve.wait_ge(s_br, num(g + 1))
                    exact(bt[:, 0, :], big[:, l % 2, 0:T], bt[:, 1, :], kb_free)
                    for m in range(2):
                        step(V.scalar_tensor_tensor(hn[:, m, :], hn[:, m, :], scalar(nrm[:, 4, :], g * 2 + m),
                                                    kb_free, ALU.mult, ALU.mult))
                        V.tensor_tensor(y[:, m, :], hn[:, m, :], so[:, m, :], ALU.mult).then_inc(s_by, 1)
                if r == 4 and exists(g, B_HEADS):
                    for m in range(2):
                        dve.wait_ge(s_xhi, num(X_OB + g * 2 + (m + 1)))
                        V.tensor_tensor(part(mid, g * 2 + m, 1), y[:, m, :],
                                        part(mid, g * 2 + m, 0).bitcast(F32), ALU.subtract).then_inc(s_x, 1)

            kb_free = bt[:, 0, :]

            dve.wait_ge(s_con, 96)
            for n in range(KT):
                x_lo(n, 0, X_A)
            for i in range(20):
                split(i, i)
                if i == 0:
                    for n in range(6):
                        src = trig[:, n % 2 if n < 4 else 2 + n % 2, :]
                        step(V.tensor_scalar(tab[:, n, :], src, col[:, n:n + 1], None, ALU.mult))
                a_step(i, i)

            def a_turn(i, k):
                split(U_A + i, U_A + k)
                a_step(i, k)
            loop(dve, 20, A_N, 4, a_turn, c, A_DVE)

            def run_out(layer, U0, tail):
                def turn(i, k):
                    split(U0 + i, U0 + k)
                    out_step(i, k, layer)
                for i in range(4):
                    split(U0 + i, U0 + i)
                    tail(i)
                    out_step(i, i, layer)
                loop(dve, 4, NT, 4, turn, c, 4)

            def a_tail(i):
                for s in ((A_N,), range(A_N + 1, A_N + 7))[i] if i < 2 else ():
                    a_step(s, s)

            def b_tail(i):
                for s in ((B_N,), range(B_N + 1, B_N + 5))[i] if i < 2 else ():
                    b_step(s, s)

            def run_ffn(layer):
                for half in range(2):
                    U0 = U_F[layer] + half * (UP_N + DN_N)

                    def up(i, k):
                        split(U0 + i, U0 + k)
                        up_step(i, k, layer, half)
                    for i in range(4):
                        split(U0 + i, U0 + i)
                        if half == 0:
                            for s in ((NT,), (NT + 1, NT + 2))[i] if i < 2 else ():
                                out_step(s, s, layer)
                            if i == 2:
                                norm_factor(2 * layer + 1)
                                dve.wait_ge(s_clear, num(layer + 1))
                        else:
                            for s in ((DN_N,), (DN_N + 1,))[i] if i < 2 else ():
                                down_step(s, s, layer, 0)
                        up_step(i, i, layer, half)
                    loop(dve, 4, UP_N, 4, up, c, UP_DVE)

                    U1 = U0 + UP_N

                    def down(i, k):
                        split(U1 + i, U1 + k, PIECES_DN)
                        down_step(i, k, layer, half)
                    for i in range(4):
                        split(U1 + i, U1 + i, PIECES_DN)
                        for s in ((UP_N,), (UP_N + 1, UP_N + 2))[i] if i < 2 else ():
                            up_step(s, s, layer, half)
                        down_step(i, i, layer, half)
                    loop(dve, 4, DN_N, 4, down, c, 2)

            run_out(0, U_OA, a_tail)
            run_ffn(0)
            for i in range(13):
                split(U_B + i, U_B + i)
                for s in ((DN_N,), (DN_N + 1, DN_N + 2))[i] if i < 2 else ():
                    down_step(s, s, 0, 1)
                if i == 2:
                    norm_factor(2)
                b_step(i, i)

            def b_turn(i, k):
                split(U_B + i, U_B + k)
                b_step(i, k)
            loop(dve, 13, B_N, 12, b_turn, c, B_DVE)
            run_out(1, U_OB, b_tail)
            run_ffn(1)
            down_step(DN_N, DN_N, 1, 1)
            down_step(DN_N + 1, DN_N + 1, 1, 1)

        @block.tensor
        def _(pe):
            mm = nc.tensor.matmul

            def unit(U, k, x, X, first=0, bank_of=None, begin=True, end=True, pieces=PIECES):
                b = (k if bank_of is None else bank_of) % 4
                if begin and not early(U, 4):
                    pe.wait_ge(s_evac, num(U - 3))
                for p, (a, z, inc) in enumerate(pieces):
                    pe.wait_ge(s_lo, num(U * 4 + (p + 1)))
                    pe.wait_ge(s_x, num(X + first + z))
                    for n in range(a, z):
                        w = slice(n * P, (n + 1) * P)
                        mm(bank[:, b, :], whi[:, k % 2, w], x[:, first + n].rearrange("p c t -> p (c t)"),
                           start=(begin and n == 0), stop=False)
                        ins = mm(bank[:, b, T:2 * T], wlo[:, k % 2, w], x[:, first + n, 0, :],
                                 start=False, stop=(end and z == pieces[-1][1] and n == z - 1))
                    ins.then_inc(s_mm, inc)

            def norm_sum(norm):
                pe.wait_ge(s_acc, num(norm + 1))
                mm(bank[:, VAL, 0:T], ones, acc[:], start=True, stop=True).then_inc(s_nsum, 1)

            def a_stage(i, k):
                if i == 0:
                    norm_sum(0)
                if i == 1 or i == 2:
                    n = i - 1
                    pe.wait_ge(s_y, num(n + 1))
                    if n:
                        pe.wait_ge(s_krot, 1)
                    mm(bank[:, ROT, 0:T], (rot_i, rot_a)[n], y[:, n, :], start=True, stop=True)
                    pe.wait_ge(s_sq, num(n + 1))
                    mm(bank[:, ROT, T:2 * T], ones, ysq[:, n, :], start=True, stop=True).then_inc(s_rot, 1)
                if i == 3 or i == 4:
                    n = i - 3
                    width = (P, IDX_HEADS)[n]
                    pe.wait_ge(s_vy, num(n + 1))
                    if n:
                        pe.wait_ge(s_natc, 1)
                    for s in range(2):
                        ins = nc.tensor.transpose(bank[:, TRN, n * T + s * width:n * T + (s + 1) * width],
                                                  vT[0:width, n, s * P:(s + 1) * P], ident[0:width, 0:width])
                    ins.then_inc(s_nat, 1)
                if isinstance(i, int) and 5 <= i < 13:
                    t = i - 5
                    pe.wait_ge(s_y, num(t + 3))
                    if t == 0:
                        pe.wait_ge(s_krot, 2)
                    else:
                        pe.wait_ge(s_qi, num(t))
                    mm(bank[:, ROT, 0:T], rot_i, y[:, t % 2, :], start=True, stop=True).then_inc(s_rot, 1)
                if isinstance(i, int) and 6 <= i < 14:
                    t = i - 6
                    pe.wait_ge(s_qi, num(t + 1))
                    if t == 0:
                        pe.wait_ge(s_kT, 1)
                        pe.wait_ge(s_natc, 2)
                    else:
                        pe.wait_ge(s_rl, num(2 * t))
                    for m in range(2):
                        rows = slice(64 * m, 64 * m + 64)
                        for q, (a, z) in enumerate(QBLK):
                            ins = mm(bank[:, LOG + m, a:z], qT[rows, t % 2, q * P:(q + 1) * P], kiT[rows, 0:z - a],
                                     start=True, stop=True)
                        ins.then_inc(s_isc, 1)
                h, j = i - 13, k - 13
                if exists(h, A_HEADS):
                    pe.wait_ge(s_y, num(h + 11))
                    if early(h, 1):
                        pe.wait_ge(s_qi, 8)
                    else:
                        pe.wait_ge(s_qT, num(h))
                    mm(bank[:, ROT, 0:T], rot_a, y[:, j % 2, :], start=True, stop=True)
                    pe.wait_ge(s_sq, num(h + 3))
                    for q in range(2):
                        ins = mm(bank[:, ROT, T + q:T + q + 1], ysq[:, j % 2, q * P:(q + 1) * P], ones[:, 0:1],
                                 start=True, stop=True)
                    ins.then_inc(s_rot, 1)
                if exists(h - 1, A_HEADS):
                    pe.wait_ge(s_qT, num(h))
                    if early(h - 1, 1):
                        pe.wait_ge(s_rl, 16)
                        pe.wait_ge(s_kT, 2)
                    else:
                        pe.wait_ge(s_nb, num(h - 1))
                    for q, (a, z) in enumerate(QBLK):
                        ins = mm(bank[:, LOG, a:z], qT[:, (j - 1) % 2, q * P:(q + 1) * P], kT[:, 0:z - a],
                                 start=True, stop=True)
                    ins.then_inc(s_log, 1)
                if exists(h - 3, A_HEADS):
                    pe.wait_ge(s_pn, num(h - 2))
                    if not early(h - 3, 1):
                        pe.wait_ge(s_ptc, num(h - 3))
                    for s, src in enumerate((0, P, 2 * P)):
                        ins = nc.tensor.transpose(bank[:, TRN, s * P:(s + 1) * P],
                                                  pp[:, (j - 1) % 2, src:src + P], ident)
                    ins.then_inc(s_pt, 1)
                if exists(h - 4, A_HEADS):
                    pe.wait_ge(s_ptc, num(h - 3))
                    if not early(h - 4, 1):
                        pe.wait_ge(s_x, num(X_OA + (h - 4)))
                    mm(bank[:, VAL, 0:T], vN[:, 0, :], pT[:, 0:T], start=True, stop=False)
                    mm(bank[:, VAL, P:T], vN[:, 1, :], pT[:, T:3 * P], start=False, stop=True).then_inc(s_o, 1)

            def b_stage(i, k):
                if i == 0:
                    norm_sum(2)
                if i == 2:
                    pe.wait_ge(s_gd, 2)
                    for s in range(2):
                        ins = nc.tensor.transpose(bank[:, TRN, s * B_HEADS:(s + 1) * B_HEADS],
                                                  kb[0:B_HEADS, 1, s * P:(s + 1) * P], ident[0:B_HEADS, 0:B_HEADS])
                    ins.then_inc(s_gt, 1)
                for pair, when in enumerate((3, 4, 5, 5)):
                    if isinstance(i, int) and i == when:
                        if pair == 0:
                            pe.wait_ge(s_ga, 2)
                        else:
                            pe.wait_ge(s_bcc, num(2 * pair))
                        for m in range(2):
                            h = 2 * pair + m
                            mm(bank[:, (ROT, VAL)[m], :], ident[0:B_HEADS, h:h + 1].to_broadcast([B_HEADS, P]),
                               mrow[:, :], start=True, stop=True).then_inc(s_bc, 1)
                r = (k - 1) % 6
                h, j = (i - 1) // 6, (k - 1) // 6
                g = h - 1
                if r == 2 and exists(h, B_HEADS):
                    pe.wait_ge(s_bk, num(h + 1))
                    if not early(h, 1):
                        pe.wait_ge(s_bP, num(h))
                    mm(bank[:, LOG, 0:T], kb[:, 1, 0:P], qT[:, j % 2, :], start=True, stop=True)
                    mm(bank[:, LOG, T:3 * P], kb[:, 1, P:T], qT[:, j % 2, P:T], start=True, stop=True).then_inc(s_bS, 1)
                if r in (3, 4) and exists(h, B_HEADS):
                    m = r - 3
                    pe.wait_ge(s_bv, num(h * 2 + (m + 1)))
                    if early(h, 1):
                        pe.wait_ge(*((s_ga, 3), (s_bcc, B_HEADS))[m])
                    elif m == 0:
                        pe.wait_ge(s_bvn, num(h * 2 - 1))
                    else:
                        pe.wait_ge(s_bh, num(h))
                    for s in range(2):
                        ins = nc.tensor.transpose(bank[:, (TRN, VAL)[m], s * P:(s + 1) * P],
                                                  vT[:, m, s * P:(s + 1) * P], ident)
                    ins.then_inc(s_bvt, 1)
                if r == 5 and exists(h, B_HEADS):
                    pe.wait_ge(s_bvn, num(h * 2 + 2))
                    pe.wait_ge(s_bP, num(h + 1))
                    if early(h, 1):
                        pe.wait_ge(s_bcc, num(B_HEADS))
                    else:
                        pe.wait_ge(s_bx, num(h))
                    wt = big[:, j % 2, :]
                    for m in range(2):
                        v = slice(m * P, (m + 1) * P)
                        mm(bank[:, VAL, m * T:(m + 1) * T], vN2[:, 0, v], wt[:, 0:T], start=True, stop=False)
                        mm(bank[:, VAL, m * T + P:(m + 1) * T], vN2[:, 1, v], wt[:, T:3 * P], start=False, stop=True)
                    mm(bank[:, ROT, 0:T], ones, wt[:, 0:T], start=True, stop=False)
                    mm(bank[:, ROT, P:T], ones, wt[:, T:3 * P], start=False, stop=True).then_inc(s_bnum, 1)
                if r == 0 and exists(g, B_HEADS):
                    pe.wait_ge(s_bsq, num(g + 1))
                    mm(bank[:, ROT, T:2 * T], ones, ysq[:, 0, :], start=True, stop=False)
                    mm(bank[:, ROT, T:2 * T], ones, ysq[:, 1, :], start=False, stop=True).then_inc(s_bss, 1)

            for i in range(20):
                unit(i, i, xs, X_A)
                a_stage(i, i)

            def a_turn(i, k):
                unit(U_A + i, U_A + k, xs, X_A)
                a_stage(i, k)
            loop(pe, 20, A_N, 4, a_turn)
            for i in range(A_N, A_N + 5):
                a_stage(i, i)

            def run_out(U0, X0):
                loop(pe, 0, NT, 4, lambda i, k: unit(U0 + i, U0 + k, mid, X0))

            def run_ffn(layer):
                for half in range(2):
                    U0 = U_F[layer] + half * (UP_N + DN_N)
                    X1 = X_F[layer] + NT + half * HALF
                    for i in range(4):
                        unit(U0 + i, U0 + i, xs, X_F[layer])
                        if i == 0 and half == 0:
                            norm_sum(2 * layer + 1)
                    loop(pe, 4, UP_N, 4, lambda i, k: unit(U0 + i, U0 + k, xs, X_F[layer]))
                    U1 = U0 + UP_N

                    def down(i, k):
                        if k % 2 == 0:
                            unit(U1 + i, U1 + k, mid, X1, 0, U1 + k, True, False, PIECES_DN)
                        else:
                            unit(U1 + i, U1 + k, mid, X1, QRT, U1 + k - 1, False, True, PIECES_DN)
                    loop(pe, 0, DN_N, 4, down)

            run_out(U_OA, X_OA)
            run_ffn(0)
            for i in range(13):
                unit(U_B + i, U_B + i, xs, X_B)
                b_stage(i, i)

            def b_turn(i, k):
                unit(U_B + i, U_B + k, xs, X_B)
                b_stage(i, k)
            loop(pe, 13, B_N, 12, b_turn)
            b_stage(B_N, B_N)
            run_out(U_OB, X_OB)
            run_ffn(1)


A_DVE = 40
UP_DVE = 8
B_DVE = 28



def kernel(**inputs):
    import numpy as np
    import concourse.bacc as bacc
    from concourse.bass_utils import run_bass_kernel_spmd

    def blocks(w, columns, kt=KT):
        w = w[:, columns]
        return w.reshape(kt, P, -1, P).transpose(2, 1, 0, 3).reshape(-1, P, kt * P)

    span = np.arange
    arrays = {k: np.asarray(v) for k, v in inputs.items()}
    q, k, v, qi, ki, wi = 0, 2048, 2176, 2304, 3328, 3392
    a_cols = np.concatenate([span(ki, wi), span(ki, wi), span(k, qi), np.tile(span(wi, wi + IDX_HEADS), 8),
                             span(qi, ki), span(q, k)])
    i0 = 6144
    gate_rows = np.concatenate([np.tile(span(i0, i0 + 8), 4), np.tile(span(i0 + 8, i0 + 16), 4)])
    b_cols = [gate_rows, gate_rows]
    for h in range(B_HEADS):
        b_cols += [span(h * P, (h + 1) * P), 1024 + span(h * P, (h + 1) * P),
                   2048 + span(2 * h * P, 2 * (h + 1) * P), 4096 + span(2 * h * P, 2 * (h + 1) * P)]
    b_cols = np.concatenate(b_cols)

    def up_units(w):
        order = np.concatenate([c + span(f * P, (f + 1) * P) for f in range(2 * HALF) for c in (0, FF)])
        return blocks(w, order).reshape(2, UP_N, P, KT * P)

    def down_units(w):
        w = w.reshape(2, 2, QRT, P, NT, P).transpose(0, 4, 1, 3, 2, 5)
        return w.reshape(2, DN_N, P, QRT * P)

    def column(g):
        return g.reshape(-1, P).T

    eye = np.eye(P, dtype=np.float32)
    ones = np.ones((P, P), np.float32)
    swap_a, swap_i = (span(P) + 64) % P, span(P) ^ 32
    tables = []
    for dim in (P, 64):
        inv = (1.0 / (np.float32(10000.0) ** (np.arange(0, dim, 2, dtype=np.float32) / np.float32(dim)))).astype(np.float32)
        ang = np.arange(T, dtype=np.float32)[:, None] * inv[None, :]
        cos, sin = np.cos(ang).T, np.sin(ang).T
        tables += [np.tile(np.concatenate([cos, cos]), (P // dim, 1)),
                   np.tile(np.concatenate([-sin, sin]), (P // dim, 1))]
    x = arrays["x"]
    ins = {
        "xT": x[0].T,
        "a_units": blocks(arrays["a_w_in"][0], a_cols),
        "a_out": blocks(arrays["a_w_out"][0], span(D)),
        "b_units": blocks(arrays["b_w_in"][0], b_cols),
        "b_out": blocks(arrays["b_w_out"][0], span(D)),
        "f_up": np.stack([up_units(w) for w in arrays["f_w_up"]]),
        "f_down": np.stack([down_units(w) for w in arrays["f_w_down"]]),
        "consts": np.concatenate([eye, eye[swap_a], eye[swap_i], ones], axis=1),
        "tables": np.concatenate(tables, axis=1),
        "cols": np.stack([g for gain, swap in ((arrays["a_q_gain"][0], swap_a), (arrays["a_k_gain"][0], swap_a),
                                               (np.tile(arrays["a_idx_k_gain"][0], 2), swap_i))
                          for g in (gain, gain[swap])], axis=1),
        "norms": np.stack([column(g) for g in (arrays["a_norm"][0], arrays["f_norm"][0], arrays["b_norm"][0],
                                               arrays["f_norm"][1], arrays["b_head_norm"][0])], axis=1),
        "conv": np.stack([np.stack([column(w) for w in (*taps, bias)], axis=2)
                          for taps, bias in zip(arrays["f_conv_w"], arrays["f_conv_b"])], axis=1),
        "gate_bias": arrays["b_gate_bias"][0][gate_rows - i0][:, None],
    }
    nc = bacc.Bacc("TRN2", target_bir_lowering=False, num_devices=1)
    args = []
    for name, a in ins.items():
        ins[name] = a = np.ascontiguousarray(a)
        args.append(nc.dram_tensor(name, a.shape, mybir.dt.from_np(a.dtype), kind="ExternalInput").ap())
    args.append(nc.dram_tensor("outT", (D, T), F32, kind="ExternalOutput").ap())
    build(nc, *args)
    result = run_bass_kernel_spmd(nc, [ins], core_ids=[0])
    return np.ascontiguousarray(result.results[0]["outT"].T)[None]
```

```python
from contextlib import ExitStack

import concourse.bass as bass
from concourse import mybir

ALU = mybir.AluOpType
ACT = mybir.ActivationFunctionType
F32 = mybir.dt.float32
F32R = mybir.dt.float32r
AX_X = mybir.AxisListType.X

P = 128
D = 2048
T = 256
KT = D // P
NT = D // P
EPS = 1e-6
FF = 5632
HALF = FF // P // 2
QRT = HALF // 2
A_HEADS = 16
IDX_HEADS = 16
IDX_SCALE = IDX_HEADS ** -0.5 * 64 ** -0.5
N_KEEP = 64
B_HEADS = 8
LAYERS = 2

A_N = 4 + IDX_HEADS // 2 + A_HEADS
N_QI = IDX_HEADS // 2
U_KI, U_WI, U_QI = 0, 1, 2
U_K, U_V, U_Q = U_QI + N_QI, U_QI + N_QI + 1, U_QI + N_QI + 2
KEYS = (U_KI, U_K)
UP_N = 2 * HALF
DN_N = 2 * NT
B_N = 1 + 6 * B_HEADS
FFN_N = 2 * (UP_N + DN_N)
U_A = 0
U_OA = U_A + A_N
U_F0 = U_OA + NT
U_B = U_F0 + FFN_N
U_OB = U_B + B_N
U_F1 = U_OB + NT
U_F = [U_F0, U_F1]

X_A = 0
X_OA = X_A + KT
X_F0 = X_OA + A_HEADS
X_B = X_F0 + NT + 2 * HALF
X_OB = X_B + NT
X_F1 = X_OB + NT
X_F = [X_F0, X_F1]

C_F0 = A_N
C_B = C_F0 + 2 * UP_N
C_F1 = C_B + B_N
C_F = [C_F0, C_F1]

PIECES = [(0, 4, 1), (4, 8, 1), (8, 12, 1), (12, 16, 1)]
OUT_TILES = [(0, 4), (4, 8), (8, 12), (12, 15), (15, 16)]
PIECES_DN = [(0, 4, 1), (4, 8, 1), (8, QRT, 2)]

DEFERRED = {(u + n, p): u * 4 + at for u in (U_OA, U_OB)
            for at, (n, p) in enumerate(((0, 0), (0, 1), (0, 2), (1, 0), (1, 1), (1, 2), (0, 3), (1, 3)), 1)}


def multiplied(U, p=3):
    return DEFERRED.get((U, p), U * 4 + p + 1) if isinstance(U, int) else U * 4 + (p + 1)


MASKED = -3.0e38
PICKED = -3.39e38
PICKED_TEST = -3.38e38
NEG = -1e30

ROT, LOG, TRN, VAL = 4, 5, 6, 7


class Index:

    def __init__(self, turn, mult, add):
        self.turn, self.mult, self.add = turn, mult, add

    def __add__(self, n):
        return Index(self.turn, self.mult, self.add + n)

    def __sub__(self, n):
        return Index(self.turn, self.mult, self.add - n)

    def __mul__(self, n):
        return Index(self.turn, self.mult * n, self.add * n)

    def __floordiv__(self, n):
        assert self.mult % n == 0
        return Index(self.turn, self.mult // n, self.add // n)

    __radd__, __rmul__ = __add__, __mul__

    def value(self):
        scaled = self.turn * self.mult if self.mult > 1 else self.turn
        return scaled + self.add if self.add else scaled


def num(n):
    return n if isinstance(n, int) else n.value()


def exists(n, count):
    return not isinstance(n, int) or 0 <= n < count


def early(n, first):
    return isinstance(n, int) and n < first


def tile(t, n):
    return t[:, n, :] if isinstance(n, int) else t[:, bass.ds(num(n), 1), :].rearrange("p n t -> p (n t)")


def part(t, n, w):
    if isinstance(n, int):
        return t[:, n, w, :]
    return t[:, bass.ds(num(n), 1), w, :].rearrange("p n t -> p (n t)")


def scalar(t, n, *more):
    if isinstance(n, int):
        n = slice(n, n + 1)
    else:
        n = bass.ds(num(n), 1)
    if more:
        return t[:, n, more[0]:more[0] + 1].rearrange("p n m -> p (n m)")
    return t[:, n]


class Count:

    def __init__(self, eng, sem):
        self.eng, self.sem, self.done, self.shift = eng, sem, 0, 0

    def step(self, ins):
        self.done += 1
        ins.then_inc(self.sem, 1)

    def wait(self, but=0):
        self.eng.wait_ge(self.sem, num(self.shift + (self.done - but)))

    def enter(self, turn, per):
        self.first, self.per, self.shift = self.done, per, Index(turn, per, 0)

    def leave(self, turns):
        assert self.done - self.first == self.per, f"{self.done - self.first} steps in the loop, not {self.per}"
        self.done, self.shift = self.first + turns * self.per, 0


def loop(eng, start, stop, size, step, count=None, per=0):
    turns = (stop - start) // size
    assert turns * size == stop - start
    with eng.Fori(0, turns) as turn:
        if count:
            count.enter(turn, per)
        for j in range(size):
            step(Index(turn, size, start + j), start + j)
    if count:
        count.leave(turns)


def build(nc, xT, a_units, a_out, b_units, b_out, f_up, f_down, consts, tables, cols, norms, conv,
          gate_bias, out):
    with ExitStack() as ctx:
        def sb(name, shape, dt=F32):
            return ctx.enter_context(nc.sbuf_tensor(name, shape, dt))

        def sem(name):
            return ctx.enter_context(nc.semaphore(name))

        hT = sb("hT", [P, NT, T])
        xs = sb("xs", [P, KT, 2, T], F32R)
        mid = sb("mid", [P, HALF, 2, T], F32R)
        raw = sb("raw", [P, 4, KT * P])
        whi = sb("whi", [P, 2, KT * P], F32R)
        wlo = sb("wlo", [P, 2, KT * P], F32R)
        con = sb("con", [P, 2 * P])
        col = sb("col", [P, 3])
        nrm = sb("nrm", [P, 5, NT])
        cnv = sb("cnv", [P, LAYERS, 2 * HALF, 4])
        gbias = sb("gbias", [64, 1])
        cross = sb("cross", [P, 2, T])
        rB = sb("rB", [P, T])
        acc = sb("acc", [P, T])
        sqp = sb("sqp", [P, T])
        y = sb("y", [P, 2, T])
        ysq = sb("ysq", [P, 2, T])
        qT = sb("qT", [P, 2, T])
        kb = sb("kb", [P, 2, T])
        vT = sb("vT", [P, 2, T])
        hn = sb("hn", [P, 2, T])
        big = sb("big", [P, 2, 3 * P])
        sm = sb("sm", [P, 2, 8, 2])
        scr = sb("scr", [P, 24 * T])

        ident, ones = (con[:, n * P:(n + 1) * P] for n in range(2))

        def scratch(first, size):
            return scr[:, first * T:first * T + size]

        trig = scratch(0, 4 * T).rearrange("p (n t) -> p n t", n=4)
        tab = scratch(4, 6 * T).rearrange("p (n t) -> p n t", n=6)
        CQ, SQ, CK, SK, CKI, SKI = (tab[:, n, :] for n in range(6))
        kT = scratch(10, T)
        kiT = scratch(11, T)
        vN = scratch(12, T).rearrange("p (s d) -> p s d", s=2)
        rp = scratch(13, 2 * T).rearrange("p (n t) -> p n t", n=2)
        score = scratch(15, 3 * P)
        mbias = scr[:, 15 * T + 3 * P:18 * T]
        lg = scratch(18, 3 * P)
        pT = scr[:, 18 * T + 3 * P:21 * T]
        pp = scratch(21, 6 * P).rearrange("p (n t) -> p n t", n=2)
        QBLK = ((0, P), (P, 3 * P))
        wiN = sb("wiN", [P, 2, IDX_HEADS])
        mx8 = sb("mx8", [P, 2, 8])
        mbb = scratch(0, 16 * T).rearrange("p (h n t) -> p h n t", h=B_HEADS, n=2)
        vN2 = scratch(16, 2 * T).rearrange("p (s v) -> p s v", s=2)
        so = scratch(18, 2 * T).rearrange("p (n t) -> p n t", n=2)
        mrow = scr[0:B_HEADS, 20 * T:22 * T]
        bt = scratch(22, 2 * T).rearrange("p (n t) -> p n t", n=2)
        aN = sb("aN", [P, 2, B_HEADS])
        fg = scratch(0, T + 2)
        fc = scratch(2, T)
        fgl = scratch(3, T)
        fv = scratch(4, 2 * T).rearrange("p (n t) -> p n t", n=2)

        mstore = nc.dram_tensor("mstore", (B_HEADS, 2 * T), F32, kind="Internal").ap()
        bank = ctx.enter_context(nc.psum_tensor("bank", [P, 8, 2 * T], F32))

        s_raw = [sem(f"raw_loaded{n}") for n in range(4)]
        s_nrm = sem("norm_gains_loaded")
        s_con = sem("constants_loaded")
        s_tab = sem("tables_loaded")
        s_late = sem("conv_and_bias_loaded")
        s_h0 = [sem(f"x_and_unit0_loaded{n}") for n in range(4)]
        s_hi = sem("weight_hi_ready")
        s_lo = sem("weight_lo_ready")
        s_mm = sem("pieces_multiplied")
        s_cross = sem("cross_copied")
        s_evac = sem("bank_read")
        s_xhi = sem("x_hi_ready")
        s_x = sem("x_ready")
        s_h = sem("h_tile_ready")
        s_acc = sem("squares_summed")
        s_zero = sem("scores_zeroed")
        s_nsum = sem("norm_sum_ready")
        s_nx = sem("norm_mean_ready")
        s_nr = sem("norm_guess_ready")
        s_act = sem("act_steps")
        s_dve = sem("dve_steps")
        s_pool = sem("pool_steps")
        s_clear = sem("pool_cleared")
        s_fc = sem("conv_ready")
        s_fgl = sem("gelu_ready")
        s_fh = sem("gelu_value_ready")
        s_y = sem("projection_ready")
        s_vy = sem("v_wi_ready")
        s_sq = sem("projection_squared")
        s_rot = sem("projection_rotated")
        s_ss = sem("projection_square_sum")
        s_kx = sem("key_mean_ready")
        s_kr = sem("key_guess_ready")
        s_kT = sem("key_ready")
        s_nat = sem("natural_ready")
        s_natc = sem("natural_copied")
        s_isc = sem("index_products")
        s_rl = sem("index_relu")
        s_icomb = sem("index_scores_added")
        s_caus = sem("scores_causal")
        s_pick = sem("keys_picked")
        s_mask = sem("mask_ready")
        s_ms = sem("query_mean_ready")
        s_r0 = sem("query_guess_ready")
        s_log = sem("logits_ready")
        s_nb = sem("softmax_bias_ready")
        s_ex = sem("exp_ready")
        s_pn = sem("probs_ready")
        s_pt = sem("probs_transposed")
        s_ptc = sem("probs_copied")
        s_o = sem("attention_out")
        s_gd = sem("gates_dve")
        s_ga = sem("gates_act")
        s_gt = sem("gates_transposed")
        s_bst = sem("m_stored")
        s_bc0 = sem("m_broadcast_first_head")
        s_bc = sem("m_broadcast_other_heads")
        s_bq = sem("mlstm_q_ready")
        s_bk = sem("mlstm_k_ready")
        s_bv = sem("mlstm_v_ready")
        s_bvt = sem("mlstm_v_transposed")
        s_bvn = sem("mlstm_v_natural")
        s_bo = sem("mlstm_o_ready")
        s_boe = sem("mlstm_o_exp")
        s_bS = sem("mlstm_products")
        s_bE = sem("mlstm_decay")
        s_bEm = sem("mlstm_decay_causal")
        s_bP = sem("mlstm_weights")
        s_bnum = sem("mlstm_num_den")
        s_bh = sem("mlstm_h")
        s_bsq = sem("mlstm_h_squared")
        s_bsa = sem("mlstm_squares_added")
        s_bss = sem("mlstm_square_sum")
        s_bx = sem("mlstm_mean")
        s_br = sem("mlstm_guess")
        s_by = sem("mlstm_out")
        s_out = sem("output_stored")

        block = ctx.enter_context(nc.Block())

        @block.sync
        def _(sp):
            def load(src, U, k, width=KT * P):
                if not early(U, 4):
                    sp.wait_ge(s_lo, num((U - 3) * 4))
                sp.dma_start(raw[:, k % 4, 0:width], src).then_inc(s_raw[k % 4], 16)

            sp.dma_start(nrm[:], norms).then_inc(s_nrm, 16)
            for p, (a, z, _) in enumerate(PIECES):
                sp.dma_start(hT[:, a:z, :],
                             xT[a * P:z * P, :].rearrange("(k p) t -> p k t", p=P)).then_inc(s_h0[p], 16)
                sp.dma_start(raw[:, 0, a * P:z * P], a_units[0][:, a * P:z * P]).then_inc(s_h0[p], 16)
            sp.dma_start(con[:], consts).then_inc(s_con, 16)
            load(a_units[1], 1, 1)
            sp.dma_start(col[:], cols).then_inc(s_tab, 16)
            sp.dma_start(scr[:, 0:4 * T], tables).then_inc(s_tab, 16)
            load(a_units[2], 2, 2)
            load(a_units[3], 3, 3)
            sp.dma_start(cnv[:], conv).then_inc(s_late, 16)
            sp.dma_start(gbias[:], gate_bias).then_inc(s_late, 16)

            def stream(src, U0, n, width=KT * P, first=0):
                odd = (n - first) % 4
                for j in range(first, first + odd):
                    load(src[j], U0 + j, U0 + j, width)
                first += odd
                loop(sp, first, n, 4, lambda i, k: load(
                    src[bass.ds(num(i), 1)].rearrange("a p n -> (a p) n"), U0 + i, U0 + k, width))

            stream(a_units, U_A, A_N, first=4)
            stream(a_out, U_OA, NT)
            for layer in range(LAYERS):
                for half in range(2):
                    U = U_F[layer] + half * (UP_N + DN_N)
                    stream(f_up[layer, half], U, UP_N)
                    stream(f_down[layer, half], U + UP_N, DN_N, QRT * P)
                if layer == 0:
                    stream(b_units, U_B, B_N)
                    stream(b_out, U_OB, NT)
            for n, (a, z) in enumerate(OUT_TILES):
                sp.wait_ge(s_h, 3 * NT + z)
                sp.dma_start(out[a * P:z * P, :].rearrange("(k p) t -> p k t", p=P),
                             hT[:, a:z, :]).then_inc(s_out, 16)
            sp.wait_ge(s_out, 16 * len(OUT_TILES))

        @block.gpsimd
        def _(pool):
            c = Count(pool, s_pool)

            def clear():
                c.step(nc.gpsimd.memset(acc[:], 0.0))
                c.wait()

            def add_square(n):
                c.step(nc.gpsimd.tensor_tensor(sqp[:], tile(hT, n), tile(hT, n), ALU.mult))
                c.wait()
                c.step(nc.gpsimd.tensor_tensor(acc[:], acc[:], sqp[:], ALU.add))
                c.wait()

            def sum_squares(norm):
                pool.wait_ge(s_nsum, num(norm))
                clear()

                def one(n, k):
                    pool.wait_ge(s_h, num((norm - 1) * NT + 1 + n))
                    add_square(n)
                loop(pool, 0, NT, 4, one, c, 8)
                c.step(nc.gpsimd.tensor_copy(sqp[:, 0:1], acc[:, 0:1]))
                c.wait()
                nc.gpsimd.tensor_copy(sqp[:, 1:2], acc[:, 1:2]).then_inc(s_acc, 1)

            four, square = scratch(19, 4 * T), scratch(15, 4 * T)
            for p, (a, z, _) in enumerate(PIECES):
                pool.wait_ge(s_h0[p], 32)
                x4 = hT[:, a:z, :].rearrange("p n t -> p (n t)")
                if p > 1:
                    c.wait()
                c.step(nc.gpsimd.tensor_tensor(square if p else four, x4, x4, ALU.mult))
                if p:
                    c.wait()
                    c.step(nc.gpsimd.tensor_tensor(four, four, square, ALU.add))
            c.wait()
            c.step(nc.gpsimd.tensor_tensor(four[:, 0:2 * T], four[:, 0:2 * T], four[:, 2 * T:4 * T], ALU.add))
            c.wait()
            nc.gpsimd.tensor_tensor(acc[:], four[:, 0:T], four[:, T:2 * T], ALU.add).then_inc(s_acc, 1)
            nc.gpsimd.memset(score, 0.0).then_inc(s_zero, 1)

            def rotate(n, k, width, cos, sin, dst, free=None):
                pool.wait_ge(s_y, num(n + 1))
                src = y[:, k % 2, :]
                step(nc.gpsimd.tensor_tensor(rp[:, 0, :], src, cos, ALU.mult))
                half = width // 2
                for a in range(0, P, half):
                    z = a ^ half
                    step(nc.gpsimd.tensor_tensor(rp[z:z + half, 1, :], src[a:a + half], sin[a:a + half], ALU.mult))
                if free:
                    pool.wait_ge(*free)
                nc.gpsimd.tensor_tensor(dst, rp[:, 0, :], rp[:, 1, :], ALU.add).then_inc(s_rot, 1)
                pool.wait_ge(s_rot, num(n + 1))

            def step(ins):
                c.step(ins)
                c.wait()

            pool.wait_ge(s_zero, 1)
            rotate(0, 0, 64, CKI, SKI, kiT)
            for t in range(N_QI):
                rotate(t + 1, t + 1, 64, trig[:, 2, :], trig[:, 3, :], qT[:, t % 2, :],
                       (s_isc, 2 * (t - 1)) if t > 1 else None)
            rotate(N_QI + 1, 1, P, CK, SK, kT)

            def rotate_query(h, k):
                free = (s_isc, 2 * (N_QI - 1 + h)) if early(h, 2) else (s_log, num(h - 1))
                rotate(h + (N_QI + 2), k, P, CQ, SQ, qT[:, k % 2, :], free)

            pool.wait_ge(s_icomb, num(IDX_HEADS // 2))
            for d in (0, 2):
                blk = score[:, d * P:(d + 1) * P]
                nc.gpsimd.affine_select(out=blk, in_=blk, compare_op=ALU.is_ge, fill=MASKED, base=0,
                                        pattern=[[-1, P]], channel_multiplier=1).then_inc(s_caus, 1)
            pool.wait_ge(s_caus, 2)
            for h in range(3):
                rotate_query(h, h)
            pool.wait_ge(s_pick, 1)
            for d in (0, 2):
                blk = mbias[:, d * P:(d + 1) * P]
                nc.gpsimd.affine_select(out=blk, in_=blk, compare_op=ALU.is_ge, fill=NEG, base=0,
                                        pattern=[[-1, P]], channel_multiplier=1).then_inc(s_mask, 1)
            pool.wait_ge(s_mask, 2)
            for h in (3, 4, 5):
                rotate_query(h, h)
            loop(pool, 6, A_HEADS, 2, rotate_query, c, 6)
            sum_squares(1)
            pool.wait_ge(s_h, num(NT))
            nc.gpsimd.memset(fg[:, 0:2], 0.0).then_inc(s_clear, 1)
            sum_squares(2)

            def add_head_squares(g):
                pool.wait_ge(s_bsq, g + 1)
                if g:
                    pool.wait_ge(s_bss, g)
                nc.gpsimd.tensor_tensor(sqp[:], ysq[:, 0, :], ysq[:, 1, :], ALU.add).then_inc(s_bsa, 1)

            for h in range(B_HEADS):
                if h:
                    add_head_squares(h - 1)
                pool.wait_ge(s_bE, h + 1)
                for d in (0, 2):
                    blk = big[:, h % 2, d * P:(d + 1) * P]
                    nc.gpsimd.affine_select(out=blk, in_=blk, compare_op=ALU.is_ge, fill=0.0, base=0,
                                            pattern=[[1, P]], channel_multiplier=-1).then_inc(s_bEm, 1)
            add_head_squares(B_HEADS - 1)
            pool.wait_ge(s_bss, B_HEADS)
            sum_squares(3)
            nc.gpsimd.memset(fg[:, 0:2], 0.0).then_inc(s_clear, 1)

        @block.scalar
        def _(act):
            c = Count(act, s_act)

            def split(U, k, pieces=PIECES):
                if early(U, 1):
                    act.wait_ge(s_nrm, 16)
                else:
                    act.wait_ge(s_raw[k % 4], num((U - k % 4) * 4 + (16 if k % 4 else 0)))
                for p, (a, z, inc) in enumerate(pieces):
                    if early(U, 1):
                        for n in range(a, z):
                            x_hi(n, 0, s_h0[p], 32)
                    if not early(U, 2):
                        act.wait_ge(s_mm, num(multiplied(U - 2, p)))
                    nc.scalar.activation(whi[:, k % 2, a * P:z * P], raw[:, k % 4, a * P:z * P],
                                         ACT.Copy).then_inc(s_hi, inc)

            def copy_cross(U, k, i, C):
                act.wait_ge(s_mm, num(multiplied(U)))
                if not early(i, 2):
                    act.wait_ge(s_evac, num(U - 1))
                nc.scalar.activation(cross[:, C % 2, :], bank[:, k % 4, T:2 * T],
                                     ACT.Copy).then_inc(s_cross, 1)

            def x_hi(n, norm, sem, value):
                act.wait_ge(sem, num(value))
                nc.scalar.activation(part(xs, n, 0), tile(hT, n), ACT.Copy,
                                     scale=scalar(nrm[:, norm, :], n)).then_inc(s_xhi, 1)

            def guess(dst, tmp, src, done):
                c.step(nc.scalar.activation(tmp, src, ACT.Ln))
                c.wait()
                nc.scalar.activation(dst, tmp, ACT.Exp, scale=-0.5).then_inc(done, 1)

            def norm_guess(norm):
                act.wait_ge(s_nx, num(norm + 1))
                guess(kb[:, 0, :], hn[:, 1, :], hn[:, 0, :], s_nr)

            def a_step(i, k):
                if i == 3:
                    norm_guess(0)
                if exists(i - 2, A_N):
                    copy_cross(i - 2 + U_A, k - 2 + U_A, i - 2, k - 2)
                for n, U in enumerate(KEYS):
                    late = 1 - n
                    if i == U + 2 + late:
                        act.wait_ge(s_y, num((1, N_QI + 2)[n]))
                        nc.scalar.activation(ysq[:, n, :], y[:, n, :], ACT.Square).then_inc(s_sq, 1)
                    if i == U + 4 + late:
                        act.wait_ge(s_kx, num(n + 1))
                        guess(kb[:, n, :], ysq[:, n, :], hn[:, n, :], s_kr)
                if i == U_WI + 3:
                    act.wait_ge(s_nat, 1)
                    nc.scalar.activation(
                        wiN[:], bank[:, VAL, T:T + 2 * IDX_HEADS].rearrange("p (s d) -> p s d", s=2),
                        ACT.Copy).then_inc(s_natc, 1)
                if i == U_V + 3:
                    act.wait_ge(s_nat, 2)
                    nc.scalar.activation(vN[:], bank[:, VAL, 0:T].rearrange("p (s d) -> p s d", s=2),
                                         ACT.Copy).then_inc(s_natc, 1)
                if isinstance(i, int) and 0 <= i - U_QI - 4 < N_QI:
                    t = i - U_QI - 4
                    for m in range(2):
                        act.wait_ge(s_isc, num(2 * t + m + 1))
                        if t and m == 0:
                            act.wait_ge(s_icomb, num(t))
                        nc.scalar.activation(big[:, m, :], bank[:, LOG + m, 0:3 * P],
                                             ACT.Relu).then_inc(s_rl, 1)
                h, j = i - 14, k - 14
                if exists(h - 5, A_HEADS):
                    act.wait_ge(s_o, num(h - 4))
                    nc.scalar.activation(part(mid, h - 5, 0), bank[:, VAL, 0:T], ACT.Copy).then_inc(s_xhi, 1)
                if exists(h - 4, A_HEADS):
                    act.wait_ge(s_pt, num(h - 3))
                    nc.scalar.activation(pT[:], bank[:, TRN, 0:3 * P], ACT.Copy).then_inc(s_ptc, 1)
                if exists(h - 2, A_HEADS):
                    act.wait_ge(s_nb, num(h - 1))
                    if not early(h - 2, 2):
                        act.wait_ge(s_pt, num(h - 3))
                    m = sm[:, j % 2]
                    for q, (a, z) in enumerate(QBLK):
                        nc.scalar.activation(pp[:, j % 2, a:z], lg[:, a:z], ACT.Exp, bias=m[:, 4, q:q + 1],
                                             scale=m[:, 3, q:q + 1],
                                             accum_out=m[:, 5, q:q + 1]).then_inc(s_ex, 1)
                if exists(h, A_HEADS):
                    act.wait_ge(s_y, num(h + 11))
                    nc.scalar.activation(ysq[:, j % 2, :], y[:, j % 2, :], ACT.Square).then_inc(s_sq, 1)
                if exists(h - 1, A_HEADS):
                    act.wait_ge(s_ms, num(h))
                    m = sm[:, (j - 1) % 2]
                    guess(m[:, 2, :], m[:, 1, :], m[:, 0, :], s_r0)

            def out_step(i, k, layer):
                if exists(i - 3, NT):
                    x_hi(i - 3, 2 * layer + 1, s_h, 2 * layer * NT + (i - 2))

            def up_step(i, k, layer, half):
                U0, C0 = U_F[layer] + half * (UP_N + DN_N), C_F[layer] + half * UP_N
                tiles = (2 * layer + half) * HALF
                if exists(i - 2, UP_N):
                    copy_cross(U0 + i - 2, U0 + k - 2, i - 2, C0 + k - 2)
                if k % 2 == 1:
                    f = (i - 3) // 2
                    if exists(f, HALF):
                        act.wait_ge(s_fc, num(tiles + 1 + f))
                        if not early(f, 1):
                            act.wait_ge(s_fh, num(tiles + f))
                        nc.scalar.activation(fgl[:], fc[:], ACT.Gelu).then_inc(s_fgl, 1)
                else:
                    f = (i - 4) // 2
                    if exists(f, HALF):
                        act.wait_ge(s_fh, num(tiles + 1 + f))
                        nc.scalar.activation(part(mid, f, 0), fv[:, 1, :], ACT.Copy).then_inc(s_xhi, 1)

            def down_step(i, k, layer, half):
                if half and k % 2 == 0 and layer < LAYERS - 1:
                    n = (i - 4) // 2
                    if exists(n, NT):
                        x_hi(n, 2 * layer + 2, s_h, (2 * layer + 1) * NT + 1 + n)

            def b_step(i, k):
                if exists(i - 2, B_N):
                    copy_cross(U_B + i - 2, U_B + k - 2, i - 2, C_B + k - 2)
                if i == 2:
                    act.wait_ge(s_gd, 1)
                    c.step(nc.scalar.activation(ysq[0:B_HEADS, 1, :], ysq[0:B_HEADS, 0, :], ACT.Exp, scale=-1.0))
                    c.wait()
                    nc.scalar.activation(big[0:B_HEADS, 0, 0:T], ysq[0:B_HEADS, 1, :], ACT.Ln,
                                         bias=1.0).then_inc(s_ga, 1)
                if i == 3:
                    act.wait_ge(s_gd, 3)
                    nc.scalar.activation(mrow[:, T:2 * T], hn[0:B_HEADS, 1, :], ACT.Exp,
                                         scale=-1.0).then_inc(s_ga, 1)
                    act.wait_ge(s_ga, 2)
                    act.dma_start(mstore, mrow).then_inc(s_bst, 16)
                    act.wait_ge(s_bst, 16)
                    act.dma_start(mbb[:, 0].rearrange("p n t -> p (n t)"),
                                  mstore[0:1, :].broadcast_to([P, 2 * T])).then_inc(s_bc0, 16)
                    act.dma_start(mbb[:, 1:].rearrange("p h n t -> p (h n t)"),
                                  mstore[1:, :].rearrange("(o h) t -> o (h t)", o=1).broadcast_to(
                                      [P, (B_HEADS - 1) * 2 * T])).then_inc(s_bc, 16)
                if i == 4:
                    act.wait_ge(s_gt, 1)
                    nc.scalar.activation(aN[:], bank[:, TRN, 0:2 * B_HEADS].rearrange("p (s h) -> p s h", s=2),
                                         ACT.Copy).then_inc(s_ga, 1)
                r = (k - 1) % 6
                h, j = (i - 1) // 6, (k - 1) // 6
                g, l = h - 1, j - 1
                if r == 0 and exists(g, B_HEADS):
                    natural(g, 1)
                if r == 1 and exists(g, B_HEADS):
                    exp_o(g, 0)
                    act.wait_ge(s_bh, num(g + 1))
                    nc.scalar.activation(ysq[:], hn[:], ACT.Square).then_inc(s_bsq, 1)
                if r == 2 and exists(g, B_HEADS):
                    exp_o(g, 1)
                    act.wait_ge(s_bx, num(g + 1))
                    guess(big[:, l % 2, 0:T], vT_tmp, bt[:, 0, :], s_br)
                if r == 4 and exists(g, B_HEADS):
                    for m in range(2):
                        act.wait_ge(s_by, num(g * 2 + (m + 1)))
                        nc.scalar.activation(part(mid, g * 2 + m, 0), y[:, m, :], ACT.Copy).then_inc(s_xhi, 1)
                if r == 4 and exists(h, B_HEADS):
                    if early(h, 2):
                        act.wait_ge(s_ga, 3)
                        act.wait_ge(*((s_bc0, 16), (s_bc, 16))[h])
                    for q, (a, z, t0) in enumerate(((0, 2 * P, 0), (2 * P, 3 * P, P))):
                        ins = nc.scalar.activation(big[:, j % 2, a:z], part(mbb, h, 0)[:, t0:T], ACT.Exp,
                                                   scale=-1.0, bias=scalar(aN[:, q, :], h))
                        if q == 0:
                            c.step(ins)
                    ins.then_inc(s_bE, 1)
                if r == 5 and exists(h, B_HEADS):
                    natural(h, 0)

            def natural(h, m):
                act.wait_ge(s_bvt, num(h * 2 + (m + 1)))
                nc.scalar.activation(vN2[:, :, m * P:(m + 1) * P],
                                     bank[:, (TRN, VAL)[m], 0:T].rearrange("p (s v) -> p s v", s=2),
                                     ACT.Copy).then_inc(s_bvn, 1)

            def exp_o(h, m):
                act.wait_ge(s_bo, num(h * 2 + (m + 1)))
                nc.scalar.activation(so[:, m, :], so[:, m, :], ACT.Exp, scale=-1.0).then_inc(s_boe, 1)

            vT_tmp = kb[:, 0, :]

            act.preload_act_table_set("natural_log_exp_and_others")
            for i in range(20):
                split(i, i)
                a_step(i, i)

            def a_turn(i, k):
                split(U_A + i, U_A + k)
                a_step(i, k)
            loop(act, 20, A_N, 4, a_turn, c, 4)

            def run_out(layer, U0, N_before, tail):
                def turn(i, k):
                    split(U0 + i, U0 + k)
                    out_step(i, k, layer)
                for i in range(4):
                    split(U0 + i, U0 + i)
                    tail(i)
                    out_step(i, i, layer)
                loop(act, 4, NT, 4, turn)

            def a_tail(i):
                for s in ((A_N,), range(A_N + 1, A_N + 7))[i] if i < 2 else ():
                    a_step(s, s)

            def b_tail(i):
                for s in ((B_N,), range(B_N + 1, B_N + 5))[i] if i < 2 else ():
                    b_step(s, s)

            def run_ffn(layer):
                for half in range(2):
                    U0 = U_F[layer] + half * (UP_N + DN_N)

                    def up(i, k):
                        split(U0 + i, U0 + k)
                        up_step(i, k, layer, half)
                    for i in range(4):
                        split(U0 + i, U0 + i)
                        if half == 0:
                            for s in ((NT,), (NT + 1, NT + 2))[i] if i < 2 else ():
                                out_step(s, s, layer)
                            if i == 2:
                                norm_guess(2 * layer + 1)
                        up_step(i, i, layer, half)
                    loop(act, 4, UP_N, 4, up)

                    U1 = U0 + UP_N

                    def down(i, k):
                        split(U1 + i, U1 + k, PIECES_DN)
                        down_step(i, k, layer, half)
                    for i in range(4):
                        split(U1 + i, U1 + i, PIECES_DN)
                        for s in ((UP_N,), (UP_N + 1, UP_N + 2))[i] if i < 2 else ():
                            up_step(s, s, layer, half)
                        down_step(i, i, layer, half)
                    loop(act, 4, DN_N, 4, down)

            run_out(0, U_OA, A_N, a_tail)
            run_ffn(0)
            act.preload_act_table_set("natural_log_exp_and_others")
            for i in range(13):
                split(U_B + i, U_B + i)
                for s in ((DN_N,), (DN_N + 1, DN_N + 2))[i] if i < 2 else ():
                    down_step(s, s, 0, 1)
                if i == 2:
                    norm_guess(2)
                b_step(i, i)

            def b_turn(i, k):
                split(U_B + i, U_B + k)
                b_step(i, k)
            loop(act, 13, B_N, 12, b_turn, c, 4)
            run_out(1, U_OB, B_N, b_tail)
            run_ffn(1)

        @block.vector
        def _(dve):
            c = Count(dve, s_dve)
            V = nc.vector

            def split(U, k, pieces=PIECES):
                for p, (a, z, inc) in enumerate(pieces):
                    if early(U, 1):
                        for n in range(a, z):
                            x_lo(n, 0, X_A)
                    dve.wait_ge(s_hi, num(U * 4 + (p + 1)))
                    V.tensor_tensor(wlo[:, k % 2, a * P:z * P], raw[:, k % 4, a * P:z * P],
                                    whi[:, k % 2, a * P:z * P].bitcast(F32), ALU.subtract).then_inc(s_lo, inc)

            def step(ins):
                c.step(ins)
                c.wait()

            def evac(U, k, C, k2, dst, done=None, factor=1.0):
                dve.wait_ge(s_cross, num(C + 1))
                V.tensor_tensor(dst, bank[:, k % 4, 0:T], cross[:, k2 % 2, :], ALU.add).then_inc(s_evac, 1)
                dve.wait_ge(s_evac, num(U + 1))
                ins = V.scalar_tensor_tensor(dst, dst, factor, rB[:], ALU.mult, ALU.mult)
                if done is None:
                    step(ins)
                else:
                    ins.then_inc(done, 1)

            def x_lo(n, norm, X):
                dve.wait_ge(s_xhi, num(X + 1 + n))
                V.scalar_tensor_tensor(part(xs, n, 1), tile(hT, n), scalar(nrm[:, norm, :], n),
                                       part(xs, n, 0).bitcast(F32), ALU.mult, ALU.subtract).then_inc(s_x, 1)

            def exact(x, r, tmp, dst, done=None, factor=1.0):
                step(V.tensor_tensor(tmp, r, r, ALU.mult))
                step(V.tensor_tensor(tmp, tmp, x, ALU.mult))
                step(V.tensor_scalar(tmp, tmp, -0.5 * factor, 1.5 * factor, ALU.mult, ALU.add))
                ins = V.tensor_tensor(dst, r, tmp, ALU.mult)
                if done is None:
                    step(ins)
                else:
                    ins.then_inc(done, 1)

            def mean(dst, src, n, done, extra=EPS):
                V.tensor_scalar(dst, src, 1.0 / n, extra, ALU.mult, ALU.add).then_inc(done, 1)

            def norm_factor(norm):
                dve.wait_ge(s_nsum, num(norm + 1))
                mean(hn[:, 0, :], bank[:, VAL, 0:T], D, s_nx)
                dve.wait_ge(s_nr, num(norm + 1))
                exact(hn[:, 0, :], kb[:, 0, :], kb[:, 1, :], rB[:])

            def pick_keys(share):
                if share == 0:
                    dve.wait_ge(s_caus, 2)
                for n in range((3, 3, 2)[share]):
                    for q, (a, z) in enumerate(QBLK):
                        if n or share:
                            c.wait(1)
                        c.step(V.max(mx8[:, q, :], score[:, a:z]))
                    for q, (a, z) in enumerate(QBLK):
                        c.wait(1)
                        c.step(V.match_replace(score[:, a:z], mx8[:, q, :], score[:, a:z], PICKED))
                if share < 2:
                    return
                c.wait()
                V.tensor_scalar(mbias[:], score[:], PICKED_TEST, NEG, ALU.is_gt, ALU.mult).then_inc(s_pick, 1)
                dve.wait_ge(s_mask, 2)

            def probabilities(h, j):
                if exists(h - 3, A_HEADS):
                    m = sm[:, (j - 1) % 2]
                    dve.wait_ge(s_ex, num((h - 2) * 2))
                    step(V.reciprocal(m[:, 7, :], m[:, 5, :]))
                    for q, (a, z) in enumerate(QBLK):
                        ins = V.tensor_scalar(pp[:, (j - 1) % 2, a:z], pp[:, (j - 1) % 2, a:z],
                                              m[:, 7, q:q + 1], None, ALU.mult)
                        if q == 0:
                            c.step(ins)
                    ins.then_inc(s_pn, 1)

            def softmax_bias(h, j):
                if exists(h - 2, A_HEADS):
                    m = sm[:, j % 2]
                    dve.wait_ge(s_r0, num(h - 1))
                    exact(m[:, 0, :], m[:, 2, :], m[:, 1, :], m[:, 3, :], factor=P ** -0.5)
                    dve.wait_ge(s_log, num(h - 1))
                    if not early(h - 2, 1):
                        dve.wait_ge(s_ex, num((h - 2) * 2))
                    V.memset(mx8[:, 0, 0:1], 0.0)
                    for q, (a, z) in enumerate(QBLK):
                        c.step(V.tensor_tensor_reduce(lg[:, a:z], bank[:, LOG, a:z], mbias[:, a:z], 1.0, MASKED,
                                                      ALU.add, ALU.max, m[:, 6, q:q + 1]))
                    c.wait()
                    V.scalar_tensor_tensor(m[:, 4, :], m[:, 6, :], -1.0, m[:, 3, :], ALU.mult,
                                           ALU.mult).then_inc(s_nb, 1)

            def a_step(i, k):
                if i == 3:
                    norm_factor(0)
                for n, U in enumerate(KEYS):
                    late = 1 - n
                    if i == U + 2 + late:
                        if n:
                            dve.wait_ge(s_rot, N_QI)
                        evac(U, U, U, U, y[:, n, :], s_y)
                    dst = (kiT, kT)[n]
                    if i == U + 3 + late:
                        dve.wait_ge(s_ss, num(n + 1))
                        mean(hn[:, n, :], bank[:, ROT, T:2 * T], P, s_kx)
                    if i == U + 4 + late:
                        dve.wait_ge(s_kr, num(n + 1))
                        exact(hn[:, n, :], kb[:, n, :], hn[:, 1 - n, :], kb[:, n, :])
                        dve.wait_ge(s_rot, (1, N_QI + 2)[n])
                        V.tensor_tensor(dst, dst, kb[:, n, :], ALU.mult).then_inc(s_kT, 1)
                if i == U_WI + 2:
                    evac(U_WI, U_WI, U_WI, U_WI, vT[:, 1, :], s_vy, factor=IDX_SCALE)
                if i == U_V + 2:
                    evac(U_V, U_V, U_V, U_V, vT[:, 0, :], s_vy)
                t = i - U_QI - 2
                if isinstance(i, int) and 0 <= t < N_QI:
                    if t:
                        dve.wait_ge(s_rot, t)
                    evac(i - 2, i - 2, i - 2, i - 2, y[:, (t + 1) % 2, :], s_y)
                t = i - U_QI - 4
                if isinstance(i, int) and 0 <= t < N_QI:
                    if t == 0:
                        dve.wait_ge(s_natc, 1)
                        dve.wait_ge(s_zero, 1)
                    for m in range(2):
                        dve.wait_ge(s_rl, num(2 * t + m + 1))
                        for q, (a, z) in enumerate(QBLK):
                            ins = V.scalar_tensor_tensor(score[:, a:z], big[:, m, a:z],
                                                         wiN[:, q, 2 * t + m:2 * t + m + 1], score[:, a:z],
                                                         ALU.mult, ALU.add)
                            if m == 0 or q == 0:
                                step(ins)
                    ins.then_inc(s_icomb, 1)
                    dve.wait_ge(s_icomb, num(t + 1))
                h, j = i - 14, k - 14
                masked = not isinstance(h, int) or h > 2
                if masked:
                    probabilities(h, j)
                    softmax_bias(h, j)
                if exists(h, A_HEADS):
                    dve.wait_ge(s_rot, num(h + (N_QI + 1)))
                    evac(i - 2, k - 2, i - 2, k - 2, y[:, j % 2, :], s_y)
                if exists(h - 1, A_HEADS):
                    m = sm[:, (j - 1) % 2]
                    dve.wait_ge(s_ss, num(h + 2))
                    mean(m[:, 0, :], bank[:, ROT, T:T + 2], P, s_ms)
                if isinstance(i, int) and 0 <= h < 3:
                    pick_keys(h)
                if not masked:
                    softmax_bias(h, j)
                if exists(h - 5, A_HEADS):
                    dve.wait_ge(s_xhi, num(X_OA + (h - 4)))
                    V.tensor_tensor(part(mid, h - 5, 1), bank[:, VAL, 0:T], part(mid, h - 5, 0).bitcast(F32),
                                    ALU.subtract).then_inc(s_x, 1)

            def add_h(n, U_last, k, units, done):
                dve.wait_ge(s_mm, num(multiplied(U_last)))
                step(V.tensor_tensor(tile(hT, n), tile(hT, n), bank[:, k % 4, 0:T], ALU.add))
                V.tensor_tensor(tile(hT, n), tile(hT, n), bank[:, k % 4, T:2 * T],
                                ALU.add).then_inc(s_evac, units)
                dve.wait_ge(s_evac, num(U_last + 1))
                if done:
                    dve.sem_inc(s_h, 1)

            def out_step(i, k, layer):
                U0 = (U_OA, U_OB)[layer]
                if exists(i - 2, NT):
                    add_h(i - 2, U0 + i - 2, U0 + k - 2, 1, True)
                if exists(i - 3, NT):
                    x_lo(i - 3, 2 * layer + 1, X_F[layer])

            def up_step(i, k, layer, half):
                U0, C0 = U_F[layer] + half * (UP_N + DN_N), C_F[layer] + half * UP_N
                tiles = (2 * layer + half) * HALF
                X0 = X_F[layer] + NT + half * HALF
                if k % 2 == 0:
                    f = (i - 4) // 2
                    if exists(f, HALF):
                        dve.wait_ge(s_xhi, num(X0 + 1 + f))
                        V.tensor_tensor(part(mid, f, 1), fv[:, 1, :], part(mid, f, 0).bitcast(F32),
                                        ALU.subtract).then_inc(s_x, 1)
                    f = (i - 2) // 2
                    if exists(f, HALF):
                        taps = [scalar(cnv[:, layer, :, m], f + half * HALF) for m in range(4)]
                        evac(U0 + i - 2, U0 + k - 2, C0 + i - 2, C0 + k - 2, fg[:, 2:T + 2])
                        step(V.tensor_scalar(fc[:], fg[:, 0:T], taps[0], taps[3], ALU.mult, ALU.add))
                        step(V.scalar_tensor_tensor(fc[:], fg[:, 1:T + 1], taps[1], fc[:], ALU.mult, ALU.add))
                        V.scalar_tensor_tensor(fc[:], fg[:, 2:T + 2], taps[2], fc[:], ALU.mult,
                                               ALU.add).then_inc(s_fc, 1)
                else:
                    f = (i - 3) // 2
                    if exists(f, HALF):
                        evac(U0 + i - 2, U0 + k - 2, C0 + i - 2, C0 + k - 2, fv[:, 0, :])
                        dve.wait_ge(s_fgl, num(tiles + 1 + f))
                        V.tensor_tensor(fv[:, 1, :], fv[:, 0, :], fgl[:], ALU.mult).then_inc(s_fh, 1)

            def down_step(i, k, layer, half):
                U0 = U_F[layer] + half * (UP_N + DN_N) + UP_N
                final = half == 1
                if k % 2 == 1:
                    n = (i - 3) // 2
                    if exists(n, NT):
                        add_h(n, U0 + i - 2, U0 + k - 3, 2, final)
                elif final and layer < LAYERS - 1:
                    n = (i - 4) // 2
                    if exists(n, NT):
                        x_lo(n, 2 * layer + 2, X_B)

            def gates():
                G = B_HEADS
                evac(U_B, U_B, C_B, C_B, y[:, 0, :])
                li, xf, ax, l1 = hn[0:G, 0, :], hn[0:G, 1, :], ysq[0:G, 0, :], big[0:G, 0, 0:T]
                lf, B, a, M = ysq[0:G, 1, :], kb[0:G, 0, :], kb[0:G, 1, :], mrow[:, 0:T]
                step(V.tensor_scalar(li, y[0:G, 0, :], gbias[0:G, :], None, ALU.add))
                step(V.tensor_scalar(xf, y[32:32 + G, 0, :], gbias[32:32 + G, :], None, ALU.add))
                V.scalar_tensor_tensor(ax, xf, -1.0, xf, ALU.mult, ALU.max).then_inc(s_gd, 1)
                step(V.memset(vT[0:G, 1, :], 1.0))
                dve.wait_ge(s_ga, 1)
                step(V.tensor_scalar(lf, xf, 0.0, None, ALU.min))
                step(V.tensor_tensor(lf, lf, l1, ALU.subtract))
                step(V.tensor_tensor_scan(B, vT[0:G, 1, :], lf, 0.0, ALU.mult, ALU.add))
                V.tensor_tensor(a, li, B, ALU.subtract).then_inc(s_gd, 1)
                dve.wait_ge(s_gd, 2)
                step(V.tensor_tensor_scan(M, a, a, MASKED, ALU.max, ALU.max))
                V.tensor_tensor(hn[0:G, 1, :], B, M, ALU.add).then_inc(s_gd, 1)

            def b_evac(i, k, dst, done, factor=1.0):
                evac(U_B + i - 2, U_B + k - 2, C_B + i - 2, C_B + k - 2, dst, done, factor)

            def b_step(i, k):
                if i == 2:
                    gates()
                r = (k - 1) % 6
                h, j = (i - 1) // 6, (k - 1) // 6
                g, l = h - 1, j - 1
                if r == 2 and exists(h, B_HEADS):
                    b_evac(i, k, qT[:, j % 2, :], s_bq)
                if r == 3 and exists(h, B_HEADS):
                    if early(h, 1):
                        dve.wait_ge(s_gt, 1)
                    b_evac(i, k, kb[:, 1, :], s_bk, P ** -0.5)
                if r == 4 and exists(h, B_HEADS):
                    b_evac(i, k, vT[:, 0, :], s_bv)
                if r == 5 and exists(h, B_HEADS):
                    b_evac(i, k, vT[:, 1, :], s_bv)
                    dve.wait_ge(s_bS, num(h + 1))
                    dve.wait_ge(s_bEm, num(h * 2 + 2))
                    V.tensor_tensor(big[:, j % 2, :], bank[:, LOG, 0:3 * P], big[:, j % 2, :],
                                    ALU.mult).then_inc(s_bP, 1)
                if r in (0, 1) and exists(g, B_HEADS):
                    b_evac(i, k, so[:, r, :], s_bo)
                if r == 1 and exists(g, B_HEADS):
                    dve.wait_ge(s_bnum, num(g + 1))
                    step(V.tensor_tensor(bt[:, 0, :], bank[:, ROT, 0:T], part(mbb, g, 1), ALU.max))
                    step(V.scalar_tensor_tensor(bt[:, 0, :], bank[:, ROT, 0:T], -1.0, bt[:, 0, :], ALU.mult, ALU.max))
                    step(V.reciprocal(bt[:, 1, :], bt[:, 0, :]))
                    for m in range(2):
                        ins = V.tensor_tensor(hn[:, m, :], bank[:, VAL, m * T:(m + 1) * T], bt[:, 1, :], ALU.mult)
                        if m == 0:
                            c.step(ins)
                    ins.then_inc(s_bh, 1)
                if r == 2 and exists(g, B_HEADS):
                    dve.wait_ge(s_bss, num(g + 1))
                    mean(bt[:, 0, :], bank[:, ROT, T:2 * T], 2 * P, s_bx)
                if r in (2, 3) and exists(g, B_HEADS):
                    m = r - 2
                    dve.wait_ge(s_boe, num(g * 2 + (m + 1)))
                    step(V.tensor_scalar(so[:, m, :], so[:, m, :], 1.0, None, ALU.add))
                    step(V.reciprocal(so[:, m, :], so[:, m, :]))
                if r == 3 and exists(g, B_HEADS):
                    dve.wait_ge(s_br, num(g + 1))
                    exact(bt[:, 0, :], big[:, l % 2, 0:T], bt[:, 1, :], kb_free)
                    for m in range(2):
                        step(V.scalar_tensor_tensor(hn[:, m, :], hn[:, m, :], scalar(nrm[:, 4, :], g * 2 + m),
                                                    kb_free, ALU.mult, ALU.mult))
                        V.tensor_tensor(y[:, m, :], hn[:, m, :], so[:, m, :], ALU.mult).then_inc(s_by, 1)
                if r == 4 and exists(g, B_HEADS):
                    for m in range(2):
                        dve.wait_ge(s_xhi, num(X_OB + g * 2 + (m + 1)))
                        V.tensor_tensor(part(mid, g * 2 + m, 1), y[:, m, :],
                                        part(mid, g * 2 + m, 0).bitcast(F32), ALU.subtract).then_inc(s_x, 1)

            kb_free = bt[:, 0, :]

            for i in range(20):
                split(i, i)
                if i == 1:
                    dve.wait_ge(s_tab, 32)
                    for n in range(6):
                        src = trig[:, n % 2 if n < 4 else 2 + n % 2, :]
                        step(V.tensor_scalar(tab[:, n, :], src, col[:, n // 2:n // 2 + 1], None, ALU.mult))
                a_step(i, i)

            def a_turn(i, k):
                split(U_A + i, U_A + k)
                a_step(i, k)
            loop(dve, 20, A_N, 4, a_turn, c, A_DVE)

            def run_out(layer, U0, tail):
                def turn(i, k):
                    split(U0 + i, U0 + k)
                    out_step(i, k, layer)
                for i in range(4):
                    split(U0 + i, U0 + i)
                    tail(i)
                    out_step(i, i, layer)
                loop(dve, 4, NT, 4, turn, c, 4)

            def a_tail(i):
                for s in ((A_N,), range(A_N + 1, A_N + 7))[i] if i < 2 else ():
                    a_step(s, s)

            def b_tail(i):
                for s in ((B_N,), range(B_N + 1, B_N + 5))[i] if i < 2 else ():
                    b_step(s, s)

            def run_ffn(layer):
                for half in range(2):
                    U0 = U_F[layer] + half * (UP_N + DN_N)

                    def up(i, k):
                        split(U0 + i, U0 + k)
                        up_step(i, k, layer, half)
                    for i in range(4):
                        split(U0 + i, U0 + i)
                        if half == 0:
                            for s in ((NT,), (NT + 1, NT + 2))[i] if i < 2 else ():
                                out_step(s, s, layer)
                            if i == 2:
                                norm_factor(2 * layer + 1)
                                dve.wait_ge(s_late, 32)
                                dve.wait_ge(s_clear, num(layer + 1))
                        else:
                            for s in ((DN_N,), (DN_N + 1,))[i] if i < 2 else ():
                                down_step(s, s, layer, 0)
                        up_step(i, i, layer, half)
                    loop(dve, 4, UP_N, 4, up, c, UP_DVE)

                    U1 = U0 + UP_N

                    def down(i, k):
                        split(U1 + i, U1 + k, PIECES_DN)
                        down_step(i, k, layer, half)
                    for i in range(4):
                        split(U1 + i, U1 + i, PIECES_DN)
                        for s in ((UP_N,), (UP_N + 1, UP_N + 2))[i] if i < 2 else ():
                            up_step(s, s, layer, half)
                        down_step(i, i, layer, half)
                    loop(dve, 4, DN_N, 4, down, c, 2)

            run_out(0, U_OA, a_tail)
            run_ffn(0)
            for i in range(13):
                split(U_B + i, U_B + i)
                for s in ((DN_N,), (DN_N + 1, DN_N + 2))[i] if i < 2 else ():
                    down_step(s, s, 0, 1)
                if i == 2:
                    norm_factor(2)
                b_step(i, i)

            def b_turn(i, k):
                split(U_B + i, U_B + k)
                b_step(i, k)
            loop(dve, 13, B_N, 12, b_turn, c, B_DVE)
            run_out(1, U_OB, b_tail)
            run_ffn(1)
            down_step(DN_N, DN_N, 1, 1)
            down_step(DN_N + 1, DN_N + 1, 1, 1)

        @block.tensor
        def _(pe):
            mm = nc.tensor.matmul

            def unit(U, k, x, X, first=0, bank_of=None, begin=True, end=True, pieces=PIECES,
                     aside={}, only=range(4)):
                b = (k if bank_of is None else bank_of) % 4
                if begin and 0 in only and not early(U, 4):
                    pe.wait_ge(s_evac, num(U - 3))
                for p, (a, z, inc) in enumerate(pieces):
                    if p not in only:
                        continue
                    pe.wait_ge(s_lo, num(U * 4 + (p + 1)))
                    pe.wait_ge(s_x, num(X + first + z))
                    for n in range(a, z):
                        w = slice(n * P, (n + 1) * P)
                        mm(bank[:, b, :], whi[:, k % 2, w], x[:, first + n].rearrange("p c t -> p (c t)"),
                           start=(begin and n == 0), stop=False)
                        ins = mm(bank[:, b, T:2 * T], wlo[:, k % 2, w], x[:, first + n, 0, :],
                                 start=False, stop=(end and z == pieces[-1][1] and n == z - 1))
                    ins.then_inc(s_mm, inc)
                    if p in aside:
                        aside[p]()

            def norm_sum(norm):
                if norm == 0:
                    pe.wait_ge(s_con, 16)
                pe.wait_ge(s_acc, num(norm + 1))
                mm(bank[:, VAL, 0:T], ones, acc[:], start=True, stop=True).then_inc(s_nsum, 1)

            def a_stage(i, k):
                if i == 1:
                    norm_sum(0)
                for n, U in enumerate(KEYS):
                    if i == U + 2 - n:
                        pe.wait_ge(s_sq, num(n + 1))
                        if n:
                            pe.wait_ge(s_kx, 1)
                        mm(bank[:, ROT, T:2 * T], ones, ysq[:, n, :], start=True, stop=True).then_inc(s_ss, 1)
                for n, U in enumerate((U_WI, U_V)):
                    if i == U + 1:
                        width, at = ((IDX_HEADS, T), (P, 0))[n]
                        pe.wait_ge(s_vy, num(n + 1))
                        pe.wait_ge((s_nx, s_natc)[n], 1)
                        for s in range(2):
                            ins = nc.tensor.transpose(bank[:, VAL, at + s * width:at + (s + 1) * width],
                                                      vT[0:width, 1 - n, s * P:(s + 1) * P], ident[0:width, 0:width])
                        ins.then_inc(s_nat, 1)
                if isinstance(i, int) and 0 <= i - U_QI - 2 < N_QI:
                    t = i - U_QI - 2
                    pe.wait_ge(s_rot, t + 2)
                    if t == 0:
                        pe.wait_ge(s_kT, 1)
                    else:
                        pe.wait_ge(s_rl, num(2 * t))
                    for m in range(2):
                        rows = slice(64 * m, 64 * m + 64)
                        for q, (a, z) in enumerate(QBLK):
                            ins = mm(bank[:, LOG + m, a:z], qT[rows, t % 2, q * P:(q + 1) * P], kiT[rows, 0:z - a],
                                     start=True, stop=True)
                        ins.then_inc(s_isc, 1)
                h, j = i - 13, k - 13
                if exists(h - 3, A_HEADS):
                    pe.wait_ge(s_pn, num(h - 2))
                    if not early(h - 3, 1):
                        pe.wait_ge(s_ptc, num(h - 3))
                    for s, src in enumerate((0, P, 2 * P)):
                        ins = nc.tensor.transpose(bank[:, TRN, s * P:(s + 1) * P],
                                                  pp[:, (j - 1) % 2, src:src + P], ident)
                    ins.then_inc(s_pt, 1)
                if exists(h - 4, A_HEADS):
                    pe.wait_ge(s_ptc, num(h - 3))
                    if early(h - 4, 1):
                        pe.wait_ge(s_natc, 2)
                    else:
                        pe.wait_ge(s_x, num(X_OA + (h - 4)))
                    mm(bank[:, VAL, 0:T], vN[:, 0, :], pT[:, 0:T], start=True, stop=False)
                    mm(bank[:, VAL, P:T], vN[:, 1, :], pT[:, T:3 * P], start=False, stop=True).then_inc(s_o, 1)
                if exists(h - 1, A_HEADS):
                    pe.wait_ge(s_rot, num(h + (N_QI + 2)))
                    if early(h - 1, 1):
                        pe.wait_ge(s_rl, 16)
                        pe.wait_ge(s_kT, 2)
                    else:
                        pe.wait_ge(s_nb, num(h - 1))
                    for q, (a, z) in enumerate(QBLK):
                        ins = mm(bank[:, LOG, a:z], qT[:, (j - 1) % 2, q * P:(q + 1) * P], kT[:, 0:z - a],
                                 start=True, stop=True)
                    ins.then_inc(s_log, 1)
                if exists(h, A_HEADS):
                    pe.wait_ge(s_sq, num(h + 3))
                    if early(h, 1):
                        pe.wait_ge(s_kx, 2)
                    else:
                        pe.wait_ge(s_ms, num(h))
                    for q in range(2):
                        ins = mm(bank[:, ROT, T + q:T + q + 1], ysq[:, j % 2, q * P:(q + 1) * P], ones[:, 0:1],
                                 start=True, stop=True)
                    ins.then_inc(s_ss, 1)

            def b_stage(i, k):
                if i == 0:
                    norm_sum(2)
                if i == 2:
                    pe.wait_ge(s_gd, 2)
                    for s in range(2):
                        ins = nc.tensor.transpose(bank[:, TRN, s * B_HEADS:(s + 1) * B_HEADS],
                                                  kb[0:B_HEADS, 1, s * P:(s + 1) * P], ident[0:B_HEADS, 0:B_HEADS])
                    ins.then_inc(s_gt, 1)
                r = (k - 1) % 6
                h, j = (i - 1) // 6, (k - 1) // 6
                g = h - 1
                if r == 2 and exists(h, B_HEADS):
                    pe.wait_ge(s_bk, num(h + 1))
                    if not early(h, 1):
                        pe.wait_ge(s_bP, num(h))
                    mm(bank[:, LOG, 0:T], kb[:, 1, 0:P], qT[:, j % 2, :], start=True, stop=True)
                    mm(bank[:, LOG, T:3 * P], kb[:, 1, P:T], qT[:, j % 2, P:T], start=True, stop=True).then_inc(s_bS, 1)
                if r in (3, 4) and exists(h, B_HEADS):
                    m = r - 3
                    pe.wait_ge(s_bv, num(h * 2 + (m + 1)))
                    if early(h, 1):
                        pe.wait_ge(*((s_ga, 3), (s_nx, 3))[m])
                    elif m == 0:
                        pe.wait_ge(s_bvn, num(h * 2 - 1))
                    else:
                        pe.wait_ge(s_bh, num(h))
                    for s in range(2):
                        ins = nc.tensor.transpose(bank[:, (TRN, VAL)[m], s * P:(s + 1) * P],
                                                  vT[:, m, s * P:(s + 1) * P], ident)
                    ins.then_inc(s_bvt, 1)
                if r == 5 and exists(h, B_HEADS):
                    pe.wait_ge(s_bvn, num(h * 2 + 2))
                    pe.wait_ge(s_bP, num(h + 1))
                    if not early(h, 1):
                        pe.wait_ge(s_bx, num(h))
                    wt = big[:, j % 2, :]
                    for m in range(2):
                        v = slice(m * P, (m + 1) * P)
                        mm(bank[:, VAL, m * T:(m + 1) * T], vN2[:, 0, v], wt[:, 0:T], start=True, stop=False)
                        mm(bank[:, VAL, m * T + P:(m + 1) * T], vN2[:, 1, v], wt[:, T:3 * P], start=False, stop=True)
                    mm(bank[:, ROT, 0:T], ones, wt[:, 0:T], start=True, stop=False)
                    mm(bank[:, ROT, P:T], ones, wt[:, T:3 * P], start=False, stop=True).then_inc(s_bnum, 1)
                if r == 0 and exists(g, B_HEADS):
                    pe.wait_ge(s_bsa, num(g + 1))
                    mm(bank[:, ROT, T:2 * T], ones, sqp[:], start=True, stop=True).then_inc(s_bss, 1)

            unit(0, 0, xs, X_A)
            for i in range(1, 20):
                unit(i, i, xs, X_A, aside={0: lambda: a_stage(i - 1, i - 1)})

            def a_turn(i, k):
                unit(U_A + i, U_A + k, xs, X_A, aside={0: lambda: a_stage(i - 1, k - 1)})
            loop(pe, 20, A_N, 4, a_turn)

            def run_out(U0, X0, stage, first, last):
                aside = [lambda i=i: stage(i, i) for i in range(first, last)]
                for n in range(2):
                    unit(U0 + n, U0 + n, mid, X0, only=(0, 1, 2),
                         aside={p: aside[3 * n + p] for p in range(3) if 3 * n + p < len(aside)})
                for n in range(2):
                    unit(U0 + n, U0 + n, mid, X0, only=(3,))
                for n in range(2, 4):
                    unit(U0 + n, U0 + n, mid, X0)
                loop(pe, 4, NT, 4, lambda i, k: unit(U0 + i, U0 + k, mid, X0))

            def run_ffn(layer):
                for half in range(2):
                    U0 = U_F[layer] + half * (UP_N + DN_N)
                    X1 = X_F[layer] + NT + half * HALF
                    for i in range(4):
                        unit(U0 + i, U0 + i, xs, X_F[layer])
                        if i == 0 and half == 0:
                            norm_sum(2 * layer + 1)
                    loop(pe, 4, UP_N, 4, lambda i, k: unit(U0 + i, U0 + k, xs, X_F[layer]))
                    U1 = U0 + UP_N

                    def down(i, k):
                        if k % 2 == 0:
                            unit(U1 + i, U1 + k, mid, X1, 0, U1 + k, True, False, PIECES_DN)
                        else:
                            unit(U1 + i, U1 + k, mid, X1, QRT, U1 + k - 1, False, True, PIECES_DN)
                    loop(pe, 0, DN_N, 4, down)

            run_out(U_OA, X_OA, a_stage, A_N - 1, A_N + 5)
            run_ffn(0)
            unit(U_B, U_B, xs, X_B)
            for i in range(1, 13):
                unit(U_B + i, U_B + i, xs, X_B, aside={0: lambda: b_stage(i - 1, i - 1)})

            def b_turn(i, k):
                unit(U_B + i, U_B + k, xs, X_B, aside={0: lambda: b_stage(i - 1, k - 1)})
            loop(pe, 13, B_N, 12, b_turn)
            run_out(U_OB, X_OB, b_stage, B_N - 1, B_N + 1)
            run_ffn(1)


A_DVE = 32
UP_DVE = 8
B_DVE = 28



def kernel(**inputs):
    import numpy as np
    import concourse.bacc as bacc
    from concourse.bass_utils import run_bass_kernel_spmd

    def blocks(w, columns, kt=KT):
        w = w[:, columns]
        return w.reshape(kt, P, -1, P).transpose(2, 1, 0, 3).reshape(-1, P, kt * P)

    span = np.arange
    arrays = {k: np.asarray(v) for k, v in inputs.items()}
    q, k, v, qi, ki, wi = 0, 2048, 2176, 2304, 3328, 3392
    a_cols = np.concatenate([span(ki, wi), span(ki, wi), np.tile(span(wi, wi + IDX_HEADS), 8),
                             span(qi, ki), span(k, qi), span(q, k)])
    i0 = 6144
    gate_rows = np.concatenate([np.tile(span(i0, i0 + 8), 4), np.tile(span(i0 + 8, i0 + 16), 4)])
    b_cols = [gate_rows, gate_rows]
    for h in range(B_HEADS):
        b_cols += [span(h * P, (h + 1) * P), 1024 + span(h * P, (h + 1) * P),
                   2048 + span(2 * h * P, 2 * (h + 1) * P), 4096 + span(2 * h * P, 2 * (h + 1) * P)]
    b_cols = np.concatenate(b_cols)

    def up_units(w):
        order = np.concatenate([c + span(f * P, (f + 1) * P) for f in range(2 * HALF) for c in (0, FF)])
        return blocks(w, order).reshape(2, UP_N, P, KT * P)

    def down_units(w):
        w = w.reshape(2, 2, QRT, P, NT, P).transpose(0, 4, 1, 3, 2, 5)
        return w.reshape(2, DN_N, P, QRT * P)

    def column(g):
        return g.reshape(-1, P).T

    eye = np.eye(P, dtype=np.float32)
    ones = np.ones((P, P), np.float32)
    tables = []
    for dim in (P, 64):
        inv = (1.0 / (np.float32(10000.0) ** (np.arange(0, dim, 2, dtype=np.float32) / np.float32(dim)))).astype(np.float32)
        ang = np.arange(T, dtype=np.float32)[:, None] * inv[None, :]
        cos, sin = np.cos(ang).T, np.sin(ang).T
        tables += [np.tile(np.concatenate([cos, cos]), (P // dim, 1)),
                   np.tile(np.concatenate([sin, -sin]), (P // dim, 1))]
    x = arrays["x"]
    ins = {
        "xT": x[0].T,
        "a_units": blocks(arrays["a_w_in"][0], a_cols),
        "a_out": blocks(arrays["a_w_out"][0], span(D)),
        "b_units": blocks(arrays["b_w_in"][0], b_cols),
        "b_out": blocks(arrays["b_w_out"][0], span(D)),
        "f_up": np.stack([up_units(w) for w in arrays["f_w_up"]]),
        "f_down": np.stack([down_units(w) for w in arrays["f_w_down"]]),
        "consts": np.concatenate([eye, ones], axis=1),
        "tables": np.concatenate(tables, axis=1),
        "cols": np.stack([arrays["a_q_gain"][0], arrays["a_k_gain"][0], np.tile(arrays["a_idx_k_gain"][0], 2)],
                         axis=1),
        "norms": np.stack([column(g) for g in (arrays["a_norm"][0], arrays["f_norm"][0], arrays["b_norm"][0],
                                               arrays["f_norm"][1], arrays["b_head_norm"][0])], axis=1),
        "conv": np.stack([np.stack([column(w) for w in (*taps, bias)], axis=2)
                          for taps, bias in zip(arrays["f_conv_w"], arrays["f_conv_b"])], axis=1),
        "gate_bias": arrays["b_gate_bias"][0][gate_rows - i0][:, None],
    }
    nc = bacc.Bacc("TRN2", target_bir_lowering=False, num_devices=1)
    args = []
    for name, a in ins.items():
        ins[name] = a = np.ascontiguousarray(a)
        args.append(nc.dram_tensor(name, a.shape, mybir.dt.from_np(a.dtype), kind="ExternalInput").ap())
    args.append(nc.dram_tensor("outT", (D, T), F32, kind="ExternalOutput").ap())
    build(nc, *args)
    result = run_bass_kernel_spmd(nc, [ins], core_ids=[0])
    return np.ascontiguousarray(result.results[0]["outT"].T)[None]
```
